# Optimizing a Trainium2 kernel written in Bass

```python
import jax, jax.numpy as jnp
from jax import lax
import numpy as np
import math

D_MODEL = 2048
BATCH = 1
SEQ = 256
DEPTH = 1

GRID_W = 64
N_META = 16
EPS = 1e-6
NEG_INF = -1e30
NA_HEADS = 8
NA_HEAD_DIM = 128
NA_WIN_ROWS = 8
NA_WIN_COLS = 16
NA_COL_BLOCK = 16
NA_KEY_COLS = NA_COL_BLOCK + NA_WIN_COLS
MLA_HEADS = 8
MLA_Q_RANK = 512
MLA_KV_RANK = 256
MLA_NOPE_DIM = 128
MLA_ROPE_DIM = 64
MLA_V_DIM = 128
MLA_QK_DIM = MLA_NOPE_DIM + MLA_ROPE_DIM
ROPE_THETA = 10000.0
Q_BLOCK = 128
D_FF = 5632
CONV_W = 3

NA_WIDTH = NA_HEADS * NA_HEAD_DIM
MLA_WIDTH = MLA_HEADS * MLA_V_DIM
D_MIX = NA_WIDTH + MLA_WIDTH
IN_COLS = 3 * NA_WIDTH + MLA_Q_RANK + MLA_KV_RANK + MLA_ROPE_DIM
IN_SPLITS = [NA_WIDTH, 2 * NA_WIDTH, 3 * NA_WIDTH, 3 * NA_WIDTH + MLA_Q_RANK, 3 * NA_WIDTH + MLA_Q_RANK + MLA_KV_RANK]


def rmsnorm(x, g):
    xf = x.astype(jnp.float32)
    y = xf * lax.rsqrt(jnp.mean(xf * xf, axis=-1, keepdims=True) + EPS)
    return (y * g.astype(jnp.float32)).astype(x.dtype)

def rope_tables(length, dtype):
    inv = ROPE_THETA ** (-jnp.arange(0, MLA_ROPE_DIM, 2, dtype=jnp.float32) / MLA_ROPE_DIM)
    ang = jnp.arange(length, dtype=jnp.float32)[:, None] * inv[None, :]
    return jnp.cos(ang)[:, None, :].astype(dtype), jnp.sin(ang)[:, None, :].astype(dtype)

def apply_rope(x, cos, sin):
    half = x.shape[-1] // 2
    x1, x2 = x[..., :half], x[..., half:]
    return jnp.concatenate([x1 * cos - x2 * sin, x2 * cos + x1 * sin], axis=-1)

def neighbourhood_attention(q, k, v, rpb, meta_bias):
    B, L, H, D = q.shape
    T = L - N_META
    rows = T // GRID_W
    kh = min(NA_WIN_ROWS, rows)
    scale = D ** -0.5
    n_cb = GRID_W // NA_COL_BLOCK
    qm, km, vm = q[:, :N_META], k[:, :N_META], v[:, :N_META]

    s_mm = jnp.einsum('bqhd,bkhd->bhqk', qm, km).astype(jnp.float32) * scale + meta_bias.astype(jnp.float32)[None, :, None, :]
    p_mm = jax.nn.softmax(s_mm, axis=-1).astype(vm.dtype)
    meta_out = jnp.einsum('bhqk,bkhd->bqhd', p_mm, vm)

    qg = q[:, N_META:].reshape(B, rows, GRID_W, H, D)
    kg = k[:, N_META:].reshape(B, rows, GRID_W, H, D)
    vg = v[:, N_META:].reshape(B, rows, GRID_W, H, D)

    qcols = np.arange(GRID_W).reshape(n_cb, NA_COL_BLOCK)
    col_start = np.clip(qcols - NA_WIN_COLS // 2, 0, GRID_W - NA_WIN_COLS)
    kblk_start = np.clip(np.arange(n_cb) * NA_COL_BLOCK - NA_WIN_COLS // 2, 0, GRID_W - NA_KEY_COLS)
    key_cols = kblk_start[:, None] + np.arange(NA_KEY_COLS)[None, :]
    col_valid = (key_cols[:, None, :] >= col_start[:, :, None]) & (key_cols[:, None, :] < col_start[:, :, None] + NA_WIN_COLS)
    col_mask = jnp.asarray(np.where(col_valid, 0.0, NEG_INF), jnp.float32)
    dc_idx = np.clip(key_cols[:, None, :] - qcols[:, :, None] + NA_WIN_COLS - 1, 0, 2 * NA_WIN_COLS - 2)
    rpb32 = rpb.astype(jnp.float32)
    mbias = meta_bias.astype(jnp.float32)[None, None, None]

    def row_block(r):
        rs = jnp.clip(r - kh // 2, 0, rows - kh)
        kb = lax.dynamic_slice_in_dim(kg, rs, kh, axis=1)[:, :, key_cols]
        vb = lax.dynamic_slice_in_dim(vg, rs, kh, axis=1)[:, :, key_cols]
        qr = lax.dynamic_index_in_dim(qg, r, axis=1, keepdims=False).reshape(B, n_cb, NA_COL_BLOCK, H, D)
        s_win = jnp.einsum('bjqhd,bijkhd->bjqhik', qr, kb).astype(jnp.float32) * scale
        dr_idx = rs + jnp.arange(kh) - r + NA_WIN_ROWS - 1
        bias = rpb32[:, dr_idx][:, :, dc_idx].transpose(2, 3, 0, 1, 4)
        s_win = s_win + bias[None] + col_mask[None, :, :, None, None, :]
        s_met = jnp.einsum('bjqhd,bmhd->bjqhm', qr, km).astype(jnp.float32) * scale + mbias
        s = jnp.concatenate([s_met, s_win.reshape(B, n_cb, NA_COL_BLOCK, H, kh * NA_KEY_COLS)], axis=-1)
        p = jax.nn.softmax(s, axis=-1).astype(vb.dtype)
        p_win = p[..., N_META:].reshape(B, n_cb, NA_COL_BLOCK, H, kh, NA_KEY_COLS)
        out = jnp.einsum('bjqhm,bmhd->bjqhd', p[..., :N_META], vm) + jnp.einsum('bjqhik,bijkhd->bjqhd', p_win, vb)
        return out.reshape(B, GRID_W, H, D)

    real = lax.map(row_block, jnp.arange(rows))
    real = real.transpose(1, 0, 2, 3, 4).reshape(B, T, H, D)
    return jnp.concatenate([meta_out, real], axis=1)

def mla_attention(cq, ckv, k_pe, cq_g, ckv_g, w_q_up, w_kv_up, q_g, k_g, cos, sin):
    B, L, _ = cq.shape
    q = (rmsnorm(cq, cq_g) @ w_q_up).reshape(B, L, MLA_HEADS, MLA_QK_DIM)
    kv = (rmsnorm(ckv, ckv_g) @ w_kv_up).reshape(B, L, MLA_HEADS, MLA_NOPE_DIM + MLA_V_DIM)
    k_nope, v = kv[..., :MLA_NOPE_DIM], kv[..., MLA_NOPE_DIM:]
    k = jnp.concatenate([k_nope, jnp.broadcast_to(k_pe[:, :, None, :], (B, L, MLA_HEADS, MLA_ROPE_DIM))], axis=-1)
    q = rmsnorm(q, q_g)
    k = rmsnorm(k, k_g)
    q = jnp.concatenate([q[..., :MLA_NOPE_DIM], apply_rope(q[..., MLA_NOPE_DIM:], cos, sin)], axis=-1)
    k = jnp.concatenate([k[..., :MLA_NOPE_DIM], apply_rope(k[..., MLA_NOPE_DIM:], cos, sin)], axis=-1)
    scale = MLA_QK_DIM ** -0.5

    def attend(qb):
        s = jnp.einsum('bqhd,bkhd->bhqk', qb, k).astype(jnp.float32) * scale
        p = jax.nn.softmax(s, axis=-1).astype(v.dtype)
        return jnp.einsum('bhqk,bkhd->bqhd', p, v)

    out_meta = attend(q[:, :N_META])
    nb = (L - N_META) // Q_BLOCK
    qr = q[:, N_META:].reshape(B, nb, Q_BLOCK, MLA_HEADS, MLA_QK_DIM).transpose(1, 0, 2, 3, 4)
    out_real = lax.map(attend, qr).transpose(1, 0, 2, 3, 4).reshape(B, L - N_META, MLA_HEADS, MLA_V_DIM)
    return jnp.concatenate([out_meta, out_real], axis=1)

def conv_glu(x, w_gate, w_up, conv_w, conv_b, w_down):
    L = x.shape[1]
    g = x @ w_gate
    u = x @ w_up
    pad = CONV_W // 2
    gp = jnp.pad(g, ((0, 0), (pad, pad), (0, 0)))
    gc = conv_b
    for i in range(CONV_W):
        gc = gc + conv_w[i] * gp[:, i:i + L]
    return (jax.nn.silu(gc) * u) @ w_down

def first_inputs(seed: int = 0) -> dict:
    key = jax.random.key(seed)
    ks = jax.random.split(key, 24)
    f32 = jnp.float32

    def nrm(k, shape, s):
        return jax.random.normal(k, shape, f32) * s

    def gain(k, shape):
        return 1.0 + 0.05 * jax.random.normal(k, shape, f32)

    return {
        "x": nrm(ks[0], (BATCH, SEQ, D_MODEL), 1.0),
        "meta_tokens": nrm(ks[1], (N_META, D_MODEL), 1.0),
        "mix_norm_g": gain(ks[2], (DEPTH, D_MODEL)),
        "w_in": nrm(ks[3], (DEPTH, D_MODEL, IN_COLS), D_MODEL ** -0.5),
        "na_q_g": gain(ks[4], (DEPTH, NA_HEAD_DIM)),
        "na_k_g": gain(ks[5], (DEPTH, NA_HEAD_DIM)),
        "na_rpb": nrm(ks[6], (DEPTH, NA_HEADS, 2 * NA_WIN_ROWS - 1, 2 * NA_WIN_COLS - 1), 0.1),
        "na_meta_bias": nrm(ks[7], (DEPTH, NA_HEADS, N_META), 0.1),
        "mla_cq_g": gain(ks[8], (DEPTH, MLA_Q_RANK)),
        "mla_ckv_g": gain(ks[9], (DEPTH, MLA_KV_RANK)),
        "w_q_up": nrm(ks[10], (DEPTH, MLA_Q_RANK, MLA_HEADS * MLA_QK_DIM), MLA_Q_RANK ** -0.5),
        "w_kv_up": nrm(ks[11], (DEPTH, MLA_KV_RANK, MLA_HEADS * (MLA_NOPE_DIM + MLA_V_DIM)), MLA_KV_RANK ** -0.5),
        "mla_q_g": gain(ks[12], (DEPTH, MLA_QK_DIM)),
        "mla_k_g": gain(ks[13], (DEPTH, MLA_QK_DIM)),
        "na_out_g": gain(ks[14], (DEPTH, NA_WIDTH)),
        "mla_out_g": gain(ks[15], (DEPTH, MLA_WIDTH)),
        "w_out": nrm(ks[16], (DEPTH, D_MIX, D_MODEL), D_MIX ** -0.5),
        "ffn_norm_g": gain(ks[17], (DEPTH, D_MODEL)),
        "w_gate": nrm(ks[18], (DEPTH, D_MODEL, D_FF), D_MODEL ** -0.5),
        "w_up": nrm(ks[19], (DEPTH, D_MODEL, D_FF), D_MODEL ** -0.5),
        "conv_w": nrm(ks[20], (DEPTH, CONV_W, D_FF), CONV_W ** -0.5),
        "conv_b": nrm(ks[21], (DEPTH, D_FF), 0.01),
        "w_down": nrm(ks[22], (DEPTH, D_FF, D_MODEL), D_FF ** -0.5),
    }

def first_block(x, meta_tokens, mix_norm_g, w_in, na_q_g, na_k_g, na_rpb, na_meta_bias, mla_cq_g, mla_ckv_g,
              w_q_up, w_kv_up, mla_q_g, mla_k_g, na_out_g, mla_out_g, w_out, ffn_norm_g, w_gate, w_up,
              conv_w, conv_b, w_down):
    B = x.shape[0]
    meta = jnp.broadcast_to(meta_tokens.astype(x.dtype)[None], (B, N_META, D_MODEL))
    h = jnp.concatenate([meta, x], axis=1)
    L = h.shape[1]
    cos, sin = rope_tables(L, x.dtype)
    for l in range(DEPTH):
        hn = rmsnorm(h, mix_norm_g[l])
        proj = hn @ w_in[l]
        q_a, k_a, v_a, cq, ckv, k_pe = jnp.split(proj, IN_SPLITS, axis=-1)
        q_a = rmsnorm(q_a.reshape(B, L, NA_HEADS, NA_HEAD_DIM), na_q_g[l])
        k_a = rmsnorm(k_a.reshape(B, L, NA_HEADS, NA_HEAD_DIM), na_k_g[l])
        v_a = v_a.reshape(B, L, NA_HEADS, NA_HEAD_DIM)
        out_a = neighbourhood_attention(q_a, k_a, v_a, na_rpb[l], na_meta_bias[l]).reshape(B, L, NA_WIDTH)
        out_b = mla_attention(cq, ckv, k_pe, mla_cq_g[l], mla_ckv_g[l], w_q_up[l], w_kv_up[l],
                              mla_q_g[l], mla_k_g[l], cos, sin).reshape(B, L, MLA_WIDTH)
        mix = jnp.concatenate([rmsnorm(out_a, na_out_g[l]), rmsnorm(out_b, mla_out_g[l])], axis=-1)
        h = h + mix @ w_out[l]
        h = h + conv_glu(rmsnorm(h, ffn_norm_g[l]), w_gate[l], w_up[l], conv_w[l], conv_b[l], w_down[l])
    return h[:, N_META:]


HEAD_DIM = 128
MOBA_HEADS = 8
MOBA_BLOCK = 256
MOBA_TOPK = 3
MOBA_Q_CHUNK = 32
SB_HEADS = 8
SB_Q_BLOCK = 128
POOL_WINDOWS = (2, 4, 8, 16)
POOL_GROUPS = len(POOL_WINDOWS)
POOL_GROUP = 256
POOL_WIDTH = POOL_GROUP * POOL_GROUPS
MOBA_WIDTH = MOBA_HEADS * HEAD_DIM
SB_WIDTH = SB_HEADS * HEAD_DIM
N_BRANCH = 3
IN_WIDTH = 3 * MOBA_WIDTH + POOL_WIDTH + 3 * SB_WIDTH + N_BRANCH * D_MODEL
D_FF_2 = -(-8 * D_MODEL // (3 * 256)) * 256
REL_BUCKETS = 32
REL_MAX_EXACT = 16
REL_MAX_DIST = 2048
NEG = -1e30


def rms_norm(x, g):
    xf = x.astype(jnp.float32)
    y = xf * lax.rsqrt(jnp.mean(xf * xf, axis=-1, keepdims=True) + EPS)
    return (y * g.astype(jnp.float32)).astype(x.dtype)

def rel_bucket(dist):
    n = jnp.maximum(dist, 0)
    nf = jnp.maximum(n, 1).astype(jnp.float32)
    large = REL_MAX_EXACT + (jnp.log(nf / REL_MAX_EXACT) / math.log(REL_MAX_DIST / REL_MAX_EXACT)
                             * (REL_BUCKETS - REL_MAX_EXACT)).astype(jnp.int32)
    large = jnp.minimum(large, REL_BUCKETS - 1)
    return jnp.where(n < REL_MAX_EXACT, n, large)

def moba_attention(q, k, v, rel_table):
    B, H, S, Dh = q.shape
    nb = -(-S // MOBA_BLOCK)
    pad = nb * MOBA_BLOCK - S
    kb = jnp.pad(k, ((0, 0), (0, 0), (0, pad), (0, 0))).reshape(B, H, nb, MOBA_BLOCK, Dh)
    vb = jnp.pad(v, ((0, 0), (0, 0), (0, pad), (0, 0))).reshape(B, H, nb, MOBA_BLOCK, Dh)
    kbar = jnp.mean(kb.astype(jnp.float32), axis=3)
    topk = min(MOBA_TOPK, nb)
    scale = Dh ** -0.5
    bi = jnp.arange(B)[:, None, None, None]
    hi = jnp.arange(H)[None, :, None, None]
    hi5 = jnp.arange(H)[None, :, None, None, None]
    blk_off = jnp.arange(MOBA_BLOCK)
    Q = MOBA_Q_CHUNK

    def chunk(c):
        t0 = c * Q
        qc = lax.dynamic_slice_in_dim(q, t0, Q, axis=2).astype(jnp.float32)
        pos = t0 + jnp.arange(Q)
        own = t0 // MOBA_BLOCK
        gate = jnp.einsum('bhqd,bhnd->bhqn', qc, kbar)
        gate = jnp.where(jnp.arange(nb) < own, gate, -jnp.inf)
        _, idx = lax.top_k(gate, topk)
        valid = jnp.arange(topk) < own
        ksel = kb[bi, hi, idx].astype(jnp.float32)
        vsel = vb[bi, hi, idx].astype(jnp.float32)
        s_sel = jnp.einsum('bhqd,bhqnkd->bhqnk', qc, ksel) * scale
        key_pos = idx[..., None] * MOBA_BLOCK + blk_off
        bias_sel = rel_table[hi5, rel_bucket(pos[:, None, None] - key_pos)].astype(jnp.float32)
        s_sel = jnp.where(valid[:, None], s_sel + bias_sel, NEG)
        k_own = lax.dynamic_index_in_dim(kb, own, axis=2, keepdims=False).astype(jnp.float32)
        v_own = lax.dynamic_index_in_dim(vb, own, axis=2, keepdims=False).astype(jnp.float32)
        d_own = pos[:, None] - (own * MOBA_BLOCK + blk_off)[None, :]
        s_own = jnp.einsum('bhqd,bhkd->bhqk', qc, k_own) * scale
        s_own = jnp.where(d_own >= 0, s_own + rel_table[:, rel_bucket(d_own)].astype(jnp.float32)[None], NEG)
        logits = jnp.concatenate([s_sel.reshape(B, H, Q, topk * MOBA_BLOCK), s_own], axis=-1)
        p = jax.nn.softmax(logits, axis=-1)
        p_sel = p[..., :topk * MOBA_BLOCK].reshape(B, H, Q, topk, MOBA_BLOCK)
        p_own = p[..., topk * MOBA_BLOCK:]
        return (jnp.einsum('bhqnk,bhqnkd->bhqd', p_sel, vsel)
                + jnp.einsum('bhqk,bhkd->bhqd', p_own, v_own))

    out = lax.map(chunk, jnp.arange(S // Q))
    return jnp.moveaxis(out, 0, 2).reshape(B, H, S, Dh).astype(q.dtype)

def stick_breaking_attention(q, k, v):
    B, H, S, Dh = q.shape
    scale = Dh ** -0.5
    outs = []
    for t0 in range(0, S, SB_Q_BLOCK):
        t1 = t0 + SB_Q_BLOCK
        qc = q[:, :, t0:t1].astype(jnp.float32)
        kc = k[:, :, :t1].astype(jnp.float32)
        vc = v[:, :, :t1].astype(jnp.float32)
        z = jnp.einsum('bhqd,bhkd->bhqk', qc, kc) * scale
        causal = jnp.arange(t1)[None, :] < jnp.arange(t0, t1)[:, None]
        log_beta = jax.nn.log_sigmoid(z)
        log_1m = jnp.where(causal, jax.nn.log_sigmoid(-z), 0.0)
        after = lax.cumsum(log_1m, axis=3, reverse=True) - log_1m
        a = jnp.where(causal, jnp.exp(log_beta + after), 0.0)
        outs.append(jnp.einsum('bhqk,bhkd->bhqd', a, vc))
    return jnp.concatenate(outs, axis=2).astype(q.dtype)

def multiscale_pool(u, w_grp, scale):
    B, S, _ = u.shape
    ug = u.astype(jnp.float32).reshape(B, S, POOL_GROUPS, POOL_GROUP)
    cs = jnp.concatenate([jnp.zeros((B, 1, POOL_GROUPS, POOL_GROUP), jnp.float32),
                          jnp.cumsum(ug, axis=1)], axis=1)
    t = jnp.arange(S)
    pooled = []
    for gi, w in enumerate(POOL_WINDOWS):
        lo = jnp.maximum(t + 1 - w, 0)
        cnt = (t + 1 - lo).astype(jnp.float32)
        mean = (cs[:, 1:, gi] - cs[:, lo, gi]) / cnt[:, None]
        pooled.append(mean - ug[:, :, gi])
    p = jnp.stack(pooled, axis=2)
    y = jnp.einsum('bsgc,gcd->bsgd', p, w_grp.astype(jnp.float32)).reshape(B, S, POOL_WIDTH)
    return (y * scale.astype(jnp.float32)).astype(u.dtype)

def hybrid_mixer(h, w_in, w_pool, pool_scale, w_br_a, w_br_b, w_br_c, w_out, rel_table):
    B, S, _ = h.shape
    proj = h @ w_in
    offs = np.cumsum([MOBA_WIDTH, MOBA_WIDTH, MOBA_WIDTH, POOL_WIDTH, SB_WIDTH, SB_WIDTH, SB_WIDTH]).tolist()
    qa, ka, va, u, qs, ks, vs, gates = jnp.split(proj, offs, axis=-1)
    to_heads = lambda t, nh: t.reshape(B, S, nh, HEAD_DIM).transpose(0, 2, 1, 3)
    from_heads = lambda t: t.transpose(0, 2, 1, 3).reshape(B, S, -1)
    ya = from_heads(moba_attention(to_heads(qa, MOBA_HEADS), to_heads(ka, MOBA_HEADS),
                                   to_heads(va, MOBA_HEADS), rel_table))
    yb = multiscale_pool(u, w_pool, pool_scale)
    yc = from_heads(stick_breaking_attention(to_heads(qs, SB_HEADS), to_heads(ks, SB_HEADS),
                                             to_heads(vs, SB_HEADS)))
    g = jax.nn.sigmoid(gates.astype(jnp.float32)).reshape(B, S, N_BRANCH, D_MODEL)
    m = (g[:, :, 0] * (ya @ w_br_a).astype(jnp.float32)
         + g[:, :, 1] * (yb @ w_br_b).astype(jnp.float32)
         + g[:, :, 2] * (yc @ w_br_c).astype(jnp.float32))
    return m.astype(h.dtype) @ w_out

def swiglu(h, w_gate, w_up, w_down):
    return (jax.nn.silu(h @ w_gate) * (h @ w_up)) @ w_down

def second_inputs(seed: int = 0) -> dict:
    key = jax.random.key(seed)
    ks = jax.random.split(key, 16)
    nrm = lambda k, shape, fan: jax.random.normal(k, shape, jnp.float32) * (fan ** -0.5)
    return {
        "x": jax.random.normal(ks[0], (BATCH, SEQ, D_MODEL), jnp.float32),
        "norm_mix": 1.0 + 0.02 * jax.random.normal(ks[1], (DEPTH, D_MODEL), jnp.float32),
        "norm_ffn": 1.0 + 0.02 * jax.random.normal(ks[2], (DEPTH, D_MODEL), jnp.float32),
        "w_in": nrm(ks[3], (DEPTH, D_MODEL, IN_WIDTH), D_MODEL),
        "w_pool": nrm(ks[4], (DEPTH, POOL_GROUPS, POOL_GROUP, POOL_GROUP), POOL_GROUP),
        "pool_scale": 1.0 + 0.02 * jax.random.normal(ks[5], (DEPTH, POOL_WIDTH), jnp.float32),
        "w_br_a": nrm(ks[6], (DEPTH, MOBA_WIDTH, D_MODEL), MOBA_WIDTH),
        "w_br_b": nrm(ks[7], (DEPTH, POOL_WIDTH, D_MODEL), POOL_WIDTH),
        "w_br_c": nrm(ks[8], (DEPTH, SB_WIDTH, D_MODEL), SB_WIDTH),
        "w_out": nrm(ks[9], (DEPTH, D_MODEL, D_MODEL), D_MODEL),
        "w_gate": nrm(ks[10], (DEPTH, D_MODEL, D_FF_2), D_MODEL),
        "w_up": nrm(ks[11], (DEPTH, D_MODEL, D_FF_2), D_MODEL),
        "w_down": nrm(ks[12], (DEPTH, D_FF_2, D_MODEL), D_FF_2),
        "rel_bias": 0.5 * jax.random.normal(ks[13], (MOBA_HEADS, REL_BUCKETS), jnp.float32),
        "norm_final": 1.0 + 0.02 * jax.random.normal(ks[14], (D_MODEL,), jnp.float32),
    }

def second_block(x, norm_mix, norm_ffn, w_in, w_pool, pool_scale, w_br_a, w_br_b, w_br_c,
              w_out, w_gate, w_up, w_down, rel_bias, norm_final):
    h = x
    for l in range(DEPTH):
        h = h + hybrid_mixer(rms_norm(h, norm_mix[l]), w_in[l], w_pool[l], pool_scale[l],
                             w_br_a[l], w_br_b[l], w_br_c[l], w_out[l], rel_bias)
        h = h + swiglu(rms_norm(h, norm_ffn[l]), w_gate[l], w_up[l], w_down[l])
    return rms_norm(h, norm_final)


def setup_inputs(seed=0):
    out = dict(first_inputs(seed))
    for name, value in second_inputs(seed + 1).items():
        if name != "x":
            out[name + "_2"] = value
    return out


def reference(
    x, meta_tokens, mix_norm_g, w_in, na_q_g, na_k_g, na_rpb, na_meta_bias, mla_cq_g, mla_ckv_g,
    w_q_up, w_kv_up, mla_q_g, mla_k_g, na_out_g, mla_out_g, w_out, ffn_norm_g, w_gate, w_up,
    conv_w, conv_b, w_down, norm_mix_2, norm_ffn_2, w_in_2, w_pool_2, pool_scale_2, w_br_a_2,
    w_br_b_2, w_br_c_2, w_out_2, w_gate_2, w_up_2, w_down_2, rel_bias_2, norm_final_2,
):
    x = first_block(
        x, meta_tokens, mix_norm_g, w_in, na_q_g, na_k_g, na_rpb, na_meta_bias, mla_cq_g,
        mla_ckv_g, w_q_up, w_kv_up, mla_q_g, mla_k_g, na_out_g, mla_out_g, w_out, ffn_norm_g,
        w_gate, w_up, conv_w, conv_b, w_down,
    )
    return second_block(
        x, norm_mix_2, norm_ffn_2, w_in_2, w_pool_2, pool_scale_2, w_br_a_2, w_br_b_2, w_br_c_2,
        w_out_2, w_gate_2, w_up_2, w_down_2, rel_bias_2, norm_final_2,
    )


_drawn_inputs = setup_inputs


def setup_inputs(seed=0):
    import zlib

    import numpy as np

    out = dict(_drawn_inputs(seed))
    spreads = {}
    factors = {'conv_b': 8.0,
     'norm_mix_2': 6.208,
     'norm_ffn_2': 17.829,
     'pool_scale_2': 8.0,
     'norm_final_2': 7.919,
     'rel_bias_2': 4.884}
    for name, (base, spread) in spreads.items():
        noise = np.random.default_rng([zlib.crc32(name.encode()), seed]).standard_normal(out[name].shape)
        drawn = base * np.exp(spread * noise) if base else spread * noise
        out[name] = __import__('jax').numpy.asarray(drawn.astype(out[name].dtype))
    for name, factor in factors.items():
        out[name] = (out[name] * factor).astype(out[name].dtype)
    return out
```

```python
from contextlib import ExitStack

import numpy as np

import concourse.bass as bass
from concourse import mybir

F32 = mybir.dt.float32
F32R = mybir.dt.float32r
ACT = mybir.ActivationFunctionType
ALU = mybir.AluOpType
AX_X = mybir.AxisListType.X

P = 128
D = 2048
DB = D // P
META = 16
SEQ = 256
L = META + SEQ
Q0 = META - 2
NQ = L - Q0
QT = 3
QR = NQ // QT
HEADS = 8
EPS = 1e-6
NEG = -1e30
FF = 5632
FFB = FF // P
GRID = 64
ROWS = SEQ // GRID
RPR, RPW = 15, 2 * GRID - 1
ROPE = 64
CQB, CKVB = 4, 2
MLA_QK = 192
WINDOWS = (2, 4, 8, 16)
DISTS = 2 * SEQ - 1
BUCKETS = 32

GC = 512
CE = 1024
RING = 4
AHEAD = 2
CD = DB // 2
CF = FFB // 2
CH = HEADS // 2

VEC_SIZES = dict(mix_g=DB, ffn_g=DB, conv_w=3 * FFB, conv_b=FFB, cq_g=CQB, ckv_g=CKVB, na_q_g=1,
                 na_k_g=1, q_nope_g=1, q_rope_g=1, k_nope_g=1, k_rope_g=1, out_g=DB, mix2_g=DB,
                 ffn2_g=DB, final_g=DB, pool_scale=HEADS)
VEC = {name: sum(list(VEC_SIZES.values())[:i]) for i, name in enumerate(VEC_SIZES)}
NVEC = sum(VEC_SIZES.values())


class At:

    def __init__(self, n=0, g=0):
        self.n, self.g = n, g

    def past(self, chunks, groups):
        return At(self.n + chunks, self.g + groups)


class Turn:

    def __init__(self, at, i, chunks, groups):
        assert chunks % RING == 0
        self.first, self.i, self.chunks, self.groups = at, i, chunks, groups


def chunks_behind(at, j=0):
    return at.n + j if isinstance(at, At) else at.i * at.chunks + (at.first.n + j)


def groups_behind(at, per, j=0):
    return at.g * per + j if isinstance(at, At) else at.i * (at.groups * per) + (at.first.g * per + j)


def shifted(at, chunks, groups):
    if isinstance(at, At):
        return at.past(chunks, groups)
    return Turn(at.first.past(chunks, groups), at.i, at.chunks, at.groups)


def slot_of(at, j):
    return (at.n + j if isinstance(at, At) else at.first.n + j) % RING


def loads_of_slot(at, j):
    if isinstance(at, At):
        return (at.n + j) // RING + 1
    return at.i * (at.chunks // RING) + ((at.first.n + j) // RING + 1)


def build(nc, hT, wts, vecs, ident, ones, tril, triu, rot, cos, sin, rp, meta_b, na_mask, relT, onehot,
          neg, inv_count, out):
    NCH = wts.shape[0]
    dist_dram = nc.dram_tensor("distances", (P, HEADS, DISTS + 1), F32, kind="Internal").ap()
    with ExitStack() as ctx:
        def sb(name, shape, dt=F32):
            return ctx.enter_context(nc.sbuf_tensor(name, shape, dt))

        def sem(name):
            return ctx.enter_context(nc.semaphore(name))

        h = sb("h", [P, DB, L])
        xh = sb("xh", [P, DB, L], F32R)
        xl = sb("xl", [P, DB, L], F32R)
        raw = sb("raw", [P, RING, CE])
        whi = sb("whi", [P, RING, CE], F32R)
        wlo = sb("wlo", [P, RING, CE], F32R)
        vec = sb("vec", [P, NVEC])
        ident_s = sb("ident_s", [P, P])
        ones_s = sb("ones_s", [P, P])
        rstd = sb("rstd", [P, L])
        rs_a = sb("rs_a", [P, L])
        rs_b = sb("rs_b", [P, L])
        ss = sb("ss", [P, L])
        small = sb("small", [P, 4, 3])
        quad_a = sb("quad_a", [P, 4, L])
        quad_b = sb("quad_b", [P, 4, L])
        eps_s = sb("eps_s", [P, 1])
        rot_s = sb("rot_s", [ROPE, ROPE])
        tab = sb("tab", [ROPE, 4, L])
        BIG = 90496
        arena = (nc.sbuf_usable_end - BIG) // 32 * 32
        assert nc.sbuf_base <= arena

        def at(name, offset, shape, dt=F32):
            return nc.alloc_sbuf_tensor_at(name, shape, dt, offset=arena + offset)

        qkv = at("qkv", 0, [P, 3 * HEADS, L])
        lath = at("lath", 26112, [P, 6, L], F32R)
        latl = at("latl", 32640, [P, 6, L], F32R)
        qrope = at("qrope", 39168, [ROPE, HEADS, L])
        knope = at("knope", 47872, [P, HEADS, L])
        vmla = at("vmla", 56576, [P, HEADS, L])
        qnope = at("qnope", 65280, [P, HEADS, L])
        mixh = at("mixh", 8704, [P, DB, NQ], F32R)
        mixl = at("mixl", 25216, [P, DB, NQ], F32R)
        T0 = 73984
        sq2 = at("sq2", T0, [P, 2, L])
        qn = at("qn", T0 + 2176, [P, L])
        kn = at("kn", T0 + 3264, [P, L])
        qr = at("qr", T0 + 4352, [ROPE, L])
        kr = at("kr", T0 + 5440, [ROPE, L])
        vc = at("vc", T0 + 6528, [P, L])
        vt = at("vt", T0 + 7616, [P, 3, P])
        sx = at("sx", T0 + 9152, [P, 3, L])
        pt = at("pt", T0 + 12416, [P, 3, NQ])
        sqr = at("sqr", T0 + 12416, [ROPE, L])
        qg = at("qg", T0 + 13504, [ROPE, L])
        mq = at("mq", T0, [P, 3, SEQ])
        dist = at("dist", T0, [HEADS, DISTS + 1])
        onehot_s = at("onehot_s", T0 + 2048, [BUCKETS, DISTS + 1])
        neg_s = at("neg_s", T0 + 4096, [HEADS, DISTS + 1])
        relT_s = at("relT_s", T0 + 6144, [BUCKETS, HEADS])
        bias = at("bias", 26112, [P, 3, L])
        mask_s = at("mask_s", 29376, [P, 3, L])
        bias2 = at("bias2", T0 + 4352, [P, 2, SEQ])
        acth = at("acth", 0, [P, FFB, SEQ], F32R)
        actl = at("actl", FFB * SEQ * 4, [P, FFB, SEQ], F32R)
        qkvu = at("qkvu", 0, [P, 56, SEQ])
        yah = at("yah", 57344, [P, HEADS, SEQ], F32R)
        yal = at("yal", 65536, [P, HEADS, SEQ], F32R)
        ph = at("ph", 0, [P, HEADS, SEQ], F32R)
        pl = at("pl", 8192, [P, HEADS, SEQ], F32R)
        SBN = 3 * P
        sbz = at("sbz", 16384, [P, SBN])
        sbl = at("sbl", 17920, [P, SBN])
        sbs = at("sbs", 19456, [P, SBN])
        sbv = at("sbv", 20992, [P, 2, P])
        tril_s = at("tril_s", 22016, [P, P])
        triu_s = at("triu_s", 22528, [P, P])
        invc = at("invc", 23040, [P, 4, META])
        sbq = at("sbq", T0, [P, 3, SEQ])
        ych = at("ych", 32768, [P, HEADS, SEQ], F32R)
        ycl = at("ycl", 40960, [P, HEADS, SEQ], F32R)
        ybh = at("ybh", 24576, [P, HEADS, SEQ], F32R)
        ybl = at("ybl", 49152, [P, HEADS, SEQ], F32R)
        msum = at("msum", T0, [P, DB, SEQ])
        mh = at("mh", 0, [P, DB, SEQ], F32R)
        ml = at("ml", 16384, [P, DB, SEQ], F32R)

        acc = ctx.enter_context(nc.psum_tensor("acc", [P, 4, 512], F32))
        aux = ctx.enter_context(nc.psum_tensor("aux", [P, 4, 512], F32))
        cos_s, sin_s, kpe, kpe_sq = (tab[:, k, :] for k in range(4))
        kpe_g = quad_b[0:ROPE, 3, :]

        raw_landed = [sem(f"raw_landed{s}") for s in range(RING)]
        hi_ready, lo_ready = sem("hi_ready"), sem("lo_ready")
        chunk_used = sem("chunk_used")
        block_done = sem("block_done")
        bank_free = sem("bank_free")
        consts_landed, eps_ready = sem("consts_landed"), sem("eps_ready")
        h_landed = [sem(f"h_landed{q}") for q in range(4)]
        xh_ready, sq_ready, x_ready = sem("xh_ready"), sem("sq_ready"), sem("x_ready")
        ss_sum, rstd_ready = sem("ss_sum"), sem("rstd_ready")
        lat_hi, lat_ready, lat_sum, lat_rs = sem("lat_hi"), sem("lat_ready"), sem("lat_sum"), sem("lat_rs")
        kpe_rot, kpe_ready = sem("kpe_rot"), sem("kpe_ready")
        mix_sq, mix_sum, mix_rs = sem("mix_sq"), sem("mix_sum"), sem("mix_rs")
        mix_in, mix_hi, mix_ready = sem("mix_in"), sem("mix_hi"), sem("mix_ready")
        silu_in, silu_out = sem("silu_in"), sem("silu_out")
        act_in, act_hi, act_ready = sem("act_in"), sem("act_hi"), sem("act_ready")
        bias_landed, bias_free = sem("bias_landed"), sem("bias_free")
        dist_landed, dist_sum, dist_ready, dist_stored = (
            sem("dist_landed"), sem("dist_sum"), sem("dist_ready"), sem("dist_stored"))
        pool_in, pool_hi, pool_ready = sem("pool_in"), sem("pool_hi"), sem("pool_ready")
        yb_hi, yb_ready, yc_hi, yc_ready = sem("yb_hi"), sem("yb_ready"), sem("yc_hi"), sem("yc_ready")
        ya_done, gate_out = sem("ya_done"), sem("gate_out")
        mask_landed, tables_landed = sem("mask_landed"), sem("tables_landed")
        m_in, m_hi, m_ready = sem("m_in"), sem("m_hi"), sem("m_ready")
        out_ready, stored = sem("out_ready"), sem("stored")

        STEPS = ("sq", "sums", "rs", "qk", "vt", "scores", "sx", "exp", "p", "pt", "ptc", "ptd", "pv", "out")
        S = {k: {s: sem(f"{k}_{s}") for s in STEPS} for k in ("na", "mla", "moba")}
        SB = {s: sem(f"sb_{s}") for s in ("copy", "z", "v", "zs", "ln", "sp", "cum", "u", "exp", "a", "pv", "out")}

        class Att:

            def __init__(self, kind, rows, tiles, keys, scale):
                self.kind, self.rows, self.tiles, self.keys, self.scale = kind, rows, tiles, keys, scale
                self.nq = rows * tiles
                self.kt = [(k // P, k, min(P, keys - k)) for k in range(0, keys, P)]
                self.s = S[kind]

        NA = Att("na", QR, QT, L, float(P) ** -0.5)
        MLA = Att("mla", QR, QT, L, float(MLA_QK) ** -0.5)
        MOBA = Att("moba", P, SEQ // P, SEQ, float(P) ** -0.5)

        AT_QKV = At()
        AT_CQ = AT_QKV.past(6 * CD, 6)
        AT_CKV = AT_CQ.past(CD, 1)
        AT_QUP = AT_CKV.past(CD, 1)
        AT_KVUP = AT_QUP.past(6, 4)
        AT_OUT = AT_KVUP.past(4, 4)
        AT_FFN = AT_OUT.past(4 * CD, 4)
        AT_DOWN = AT_FFN.past(11 * 2 * CD, 22)
        AT_IN2 = AT_DOWN.past(4 * CF, 4)
        AT_POOL = AT_IN2.past(14 * CD, 14)
        AT_MERGE = AT_POOL.past(2, 2)
        AT_OUT2 = AT_MERGE.past(4 * 3 * (CD + CH), 24)
        AT_FFN2 = AT_OUT2.past(4 * CD, 4)
        AT_DOWN2 = AT_FFN2.past(11 * 2 * CD, 22)
        AT_END = AT_DOWN2.past(4 * CF, 4)
        assert nc.sbuf_base <= arena
        assert AT_END.n + RING == NCH

        block = ctx.enter_context(nc.Block())

        @block.sync
        def _(sp):
            def load(n, slot):
                sp.dma_start(raw[:, slot, :], wts[bass.ds(n, 1)].rearrange("c p f -> p (c f)"))\
                    .then_inc(raw_landed[slot], 16)

            sp.dma_start(vec[:], vecs).then_inc(consts_landed, 16)
            sp.dma_start(h[:, 0:4, :], hT[:, 0:4, :]).then_inc(h_landed[0], 16)
            for s in range(RING):
                load(s, s)
            for dst, src in ((ones_s, ones), (ident_s, ident)):
                sp.dma_start(dst[:], src).then_inc(consts_landed, 16)
            sp.dma_start(tab[:, 0, :], cos).then_inc(consts_landed, 16)
            sp.dma_start(tab[:, 1, :], sin).then_inc(consts_landed, 16)
            sp.dma_start(rot_s[:], rot).then_inc(consts_landed, 16)
            with sp.Fori(1, NCH // RING) as i:
                for s in range(RING):
                    sp.wait_ge(lo_ready, i * RING + (s + 1 - RING))
                    load(i * RING + s, s)
            for q in range(4):
                sp.wait_ge(out_ready, q + 1)
                sp.dma_start(out[:, 4 * q:4 * q + 4, :], h[:, 4 * q:4 * q + 4, META:L]).then_inc(stored, 16)
            sp.wait_ge(stored, 64)

        NCONST = 6 * 16

        @block.gpsimd
        def _(pool):
            pool.dma_start(onehot_s[:], onehot).then_inc(dist_landed, 16)
            pool.dma_start(neg_s[:], neg).then_inc(dist_landed, 16)
            pool.dma_start(relT_s[:], relT).then_inc(dist_landed, 16)
            for q in range(1, 4):
                pool.dma_start(h[:, 4 * q:4 * q + 4, :], hT[:, 4 * q:4 * q + 4, :]).then_inc(h_landed[q], 16)
            pool.wait_ge(dist_ready, 1)
            pool.dma_start(dist_dram.rearrange("c h d -> h c d"), dist[:].unsqueeze(1).to_broadcast([HEADS, P, DISTS + 1]))\
                .then_inc(dist_stored, 16)
            pool.wait_ge(chunk_used, AT_OUT.n)
            pool.dma_start(mask_s[0:QR], na_mask).then_inc(mask_landed, 16)
            pool.memset(bias[:], 0.0).then_inc(bias_free, 1)
            with pool.Fori(0, HEADS) as i:
                pool.wait_ge(bias_free, i + 1)
                pool.dma_start(bias[0:QR, :, 0:META], bass.AP(meta_b.tensor, i * META, [[0, QR], [0, 3], [1, META]]))\
                    .then_inc(bias_landed, 16)
                for r in range(ROWS):
                    a = 0
                    while a < GRID:
                        q = r * GRID + a + 2
                        n = min(GRID - a, QR - q % QR)
                        src = bass.AP(rp.tensor, i * (RPR * GRID) + (a * HEADS * RPR + 7 - r) * GRID,
                                      [[HEADS * RPR * GRID, n], [GRID, ROWS], [1, GRID]])
                        dst = bias[q % QR:q % QR + n, q // QR, META:L].rearrange("p (r c) -> p r c", c=GRID)
                        pool.dma_start(dst, src).then_inc(bias_landed, 16)
                        a += n
            pool.wait_ge(dist_stored, 16)
            pool.wait_ge(chunk_used, AT_POOL.n)
            with pool.Fori(0, HEADS) as i:
                pool.wait_ge(bias_free, i + (HEADS + 1))
                for t in range(2):
                    pool.dma_start(bias2[:, t, :],
                                   bass.AP(dist_dram.tensor, i * (DISTS + 1) + (SEQ - 1 - t * P),
                                           [[HEADS * (DISTS + 1) - 1, P], [1, SEQ]])).then_inc(bias_landed, 16)
            pool.wait_ge(ya_done, HEADS + 1)
            for dst, src in ((tril_s, tril), (triu_s, triu), (invc, inv_count)):
                pool.dma_start(dst[:], src).then_inc(tables_landed, 16)

        @block.scalar
        def _(act):
            def high_parts(at, count):
                for j in range(AHEAD, AHEAD + count):
                    act.wait_ge(raw_landed[slot_of(at, j)], loads_of_slot(at, j) * 16)
                    if not (isinstance(at, At) and at.n + j < RING):
                        act.wait_ge(chunk_used, chunks_behind(at, j - RING + 1))
                    act.activation(whi[:, slot_of(at, j), :], raw[:, slot_of(at, j), :], ACT.Copy)\
                        .then_inc(hi_ready, 1)

            def inv_rms(dst, src, n_features, wait, wait_n, done):
                act.wait_ge(wait, wait_n)
                act.activation(dst, src, ACT.Ln, scale=1.0 / n_features, bias=eps_s[:, 0:1])
                act.drain()
                act.activation(dst, dst, ACT.Exp, scale=-0.5).then_inc(done, 1)

            def residual(at, b0, gain, cols, dst_cols, chunks):
                high_parts(at, chunks)
                for ob in range(4):
                    act.wait_ge(bank_free, groups_behind(at, 4, 4 + ob + 1))
                    if gain is not None:
                        act.activation(xh[:, bass.ds(b0 + ob, 1), dst_cols], h[:, bass.ds(b0 + ob, 1), cols],
                                       ACT.Copy, scale=vec[:, bass.ds(b0 + (VEC[gain] + ob), 1)])\
                            .then_inc(xh_ready, 1)
                n = cols.stop - cols.start
                act.activation(quad_b[:, :, 0:n], h[:, bass.ds(b0, 4), cols], ACT.Square).then_inc(sq_ready, 1)

            def softmax_head(a, hd, out_block):
                s = a.s
                act.wait_ge(s["sx"], hd + 1)
                for t in range(a.tiles):
                    last = act.activation(sx[0:a.rows, t, 0:a.keys], sx[0:a.rows, t, 0:a.keys], ACT.Exp,
                                          bias=small[0:a.rows, 0, t:t + 1], accum_out=small[0:a.rows, 1, t:t + 1])
                last.then_inc(s["exp"], 1)
                act.wait_ge(s["pt"], hd + 1)
                act.activation(pt[:, 0:2, 0:a.nq], aux[:, 0:2, 0:a.nq], ACT.Copy).then_inc(s["ptc"], 1)
                act.wait_ge(s["pv"], hd + 1)
                act.activation(out_block, aux[:, 3, 0:a.nq], ACT.Copy).then_inc(s["out"], 1)

            act.wait_ge(consts_landed, NCONST)
            act.wait_ge(eps_ready, 1)
            high_parts(At(-AHEAD, 0), AHEAD)
            for q in range(4):
                act.wait_ge(h_landed[q], 16)
                if q:
                    act.wait_ge(x_ready, q)
                for k in range(4):
                    act.activation(xh[:, 4 * q + k, :], h[:, 4 * q + k, :], ACT.Copy,
                                   scale=vec[:, VEC["mix_g"] + 4 * q + k:VEC["mix_g"] + 4 * q + k + 1])\
                        .then_inc(xh_ready, 1)
                act.activation(quad_b[:, :, :], h[:, 4 * q:4 * q + 4, :], ACT.Square).then_inc(sq_ready, 1)
            inv_rms(rstd[:], aux[:, 3, 0:L], D, ss_sum, 1, rstd_ready)

            high_parts(AT_QKV, CD)
            with act.Fori(1, 6) as i:
                high_parts(Turn(AT_QKV, i, CD, 1), CD)
            for at, blocks, v in ((AT_CQ, CQB, "cq_g"), (AT_CKV, CKVB, "ckv_g")):
                k0 = 0 if at is AT_CQ else CQB
                high_parts(at, CD)
                act.wait_ge(bank_free, groups_behind(at, 4, 4 + 4))
                for k in range(blocks):
                    act.activation(lath[:, k0 + k, :], quad_a[:, k, :], ACT.Copy,
                                   scale=vec[:, VEC[v] + k:VEC[v] + k + 1])
                if at is AT_CKV:
                    act.activation(kpe_g, kpe, ACT.Copy, scale=vec[0:ROPE, VEC["k_rope_g"]:VEC["k_rope_g"] + 1])
                    act.activation(kpe_sq, kpe, ACT.Square)
                act.activation(quad_b[:, 0:blocks, :], quad_a[:, 0:blocks, :], ACT.Square).then_inc(lat_hi, 1)
                inv_rms((rs_a if at is AT_CQ else rs_b)[:], aux[:, 3, 0:L], blocks * P, lat_sum,
                        1 if at is AT_CQ else 2, lat_rs)
            for g, c in enumerate((2, 2, 1, 1)):
                high_parts(AT_QUP.past(sum((2, 2, 1, 1)[:g]), g), c)
            for g in range(4):
                high_parts(AT_KVUP.past(g, g), 1)

            act.wait_ge(bank_free, 4 + 4 * AT_OUT.g)
            act.wait_ge(dist_stored, 16)
            with act.Fori(0, HEADS) as i:
                s = MLA.s
                act.activation(sq2[:, 0, :], qnope[:, bass.ds(i, 1), :].rearrange("p e n -> p (e n)"), ACT.Square)
                act.activation(sq2[:, 1, :], knope[:, bass.ds(i, 1), :].rearrange("p e n -> p (e n)"), ACT.Square)
                act.activation(sqr[:], qrope[:, bass.ds(i, 1), :].rearrange("p e n -> p (e n)"), ACT.Square)
                act.activation(qg[:], qrope[:, bass.ds(i, 1), :].rearrange("p e n -> p (e n)"), ACT.Copy,
                               scale=vec[0:ROPE, VEC["q_rope_g"]:VEC["q_rope_g"] + 1])
                act.activation(vc[:], vmla[:, bass.ds(i, 1), :].rearrange("p e n -> p (e n)"), ACT.Copy)\
                    .then_inc(s["sq"], 1)
                inv_rms(sq2[:], aux[:, 0:2, 0:L], MLA_QK, s["sums"], i + 1, s["rs"])
                act.activation(vt[:, 0:2, :].rearrange("p a b -> p (a b)"), aux[:, 3, 0:2 * P], ACT.Copy)
                act.activation(vt[0:META, 2, :], aux[0:META, 3, 2 * P:3 * P], ACT.Copy)
                softmax_head(MLA, i, qnope[:, bass.ds(i, 1), Q0:L].rearrange("p e n -> p (e n)"))
            with act.Fori(0, HEADS) as i:
                s = NA.s
                act.activation(sq2[:], qkv[:, 0:2 * HEADS, :].rearrange("p (s e) n -> p s e n", e=HEADS)
                               [:, :, bass.ds(i, 1), :].rearrange("p s e n -> p s (e n)"), ACT.Square)
                act.activation(vc[:], qkv[:, bass.ds(i + 2 * HEADS, 1), :].rearrange("p e n -> p (e n)"), ACT.Copy)\
                    .then_inc(s["sq"], 1)
                inv_rms(sq2[:], aux[:, 0:2, 0:L], P, s["sums"], i + 1, s["rs"])
                act.activation(vt[:, 0:2, :].rearrange("p a b -> p (a b)"), aux[:, 3, 0:2 * P], ACT.Copy)
                act.activation(vt[0:META, 2, :], aux[0:META, 3, 2 * P:3 * P], ACT.Copy)
                softmax_head(NA, i, qkv[:, bass.ds(i, 1), Q0:L].rearrange("p e n -> p (e n)"))

            for q in range(4):
                src = qkv if q < 2 else qnope
                if q == 0:
                    act.wait_ge(NA.s["out"], HEADS)
                    act.wait_ge(MLA.s["out"], HEADS)
                else:
                    act.wait_ge(mix_sum, q)
                act.activation(quad_b[:, :, 0:NQ], src[:, 4 * (q % 2):4 * (q % 2) + 4, Q0:L], ACT.Square)\
                    .then_inc(mix_sq, 1)
            inv_rms(rs_a[:, 0:NQ], aux[:, 0, 0:NQ], HEADS * P, mix_sum, 4, mix_rs)
            inv_rms(rs_b[:, 0:NQ], aux[:, 1, 0:NQ], HEADS * P, mix_sum, 4, mix_rs)
            for q in range(4):
                act.wait_ge(mix_in, q + 1)
                act.activation(mixh[:, 4 * q:4 * q + 4, :], quad_a[:, :, 0:NQ], ACT.Copy).then_inc(mix_hi, 1)

            with act.Fori(0, 4) as i:
                residual(Turn(AT_OUT, i, CD, 1), i * 4, "ffn_g", slice(Q0, L), slice(Q0, L), CD)
            inv_rms(rstd[:], aux[:, 3, 0:L], D, ss_sum, 2, rstd_ready)

            def ffn(start, turn0):
                with act.Fori(0, 11) as i:
                    at = Turn(start, i, 2 * CD, 2)
                    high_parts(at, CD)
                    act.wait_ge(silu_in, i + (turn0 + 1))
                    act.activation(quad_b[:, :, 0:SEQ], quad_b[:, :, 0:SEQ], ACT.Silu).then_inc(silu_out, 1)
                    high_parts(shifted(at, CD, 1), CD)
                    act.wait_ge(bank_free, groups_behind(at, 4, 4 + 8))
                    act.activation(acth[:, bass.ds(i * 4, 4), :], quad_a[:, :, 0:SEQ], ACT.Copy).then_inc(act_hi, 1)

            ffn(AT_FFN, 0)
            with act.Fori(0, 2) as i:
                for k in range(2):
                    residual(shifted(Turn(AT_DOWN, i, 2 * CF, 2), k * CF, k), i * 8 + 4 * k, "mix2_g", slice(META, L),
                             slice(0, SEQ), CF)
            inv_rms(rstd[:], aux[:, 3, 0:L], D, ss_sum, 3, rstd_ready)

            with act.Fori(0, 14) as i:
                high_parts(Turn(AT_IN2, i, CD, 1), CD)
            act.wait_ge(bank_free, 4 + 4 * AT_POOL.g)
            with act.Fori(0, HEADS) as i:
                s = MOBA.s
                act.activation(mq[:], qkvu[:, 0:3 * HEADS, :].rearrange("p (s e) n -> p s e n", e=HEADS)
                               [:, :, bass.ds(i, 1), :].rearrange("p s e n -> p s (e n)"), ACT.Copy).then_inc(s["qk"], 1)
                act.wait_ge(s["scores"], i + 1)
                act.activation(vt[:, 0:2, :].rearrange("p a b -> p (a b)"), aux[:, 3, 0:2 * P], ACT.Copy).then_inc(s["vt"], 1)
                softmax_head(MOBA, i, yah[:, bass.ds(i, 1), :].rearrange("p e n -> p (e n)"))
            for g in range(4):
                act.wait_ge(pool_in, g + 1)
                act.activation(ph[:, 2 * g:2 * g + 2, :], quad_a[:, 2:4, 0:SEQ], ACT.Copy).then_inc(pool_hi, 1)
            with act.Fori(0, HEADS) as i:
                act.activation(sbq[:], qkvu[:, 3 * HEADS:6 * HEADS, :].rearrange("p (s e) n -> p s e n", e=HEADS)
                               [:, :, bass.ds(i, 1), :].rearrange("p s e n -> p s (e n)"), ACT.Copy)\
                    .then_inc(SB["copy"], 1)
                act.wait_ge(SB["z"], i + 1)
                act.activation(sbv[:].rearrange("p a b -> p (a b)"), aux[:, 1, 0:2 * P], ACT.Copy).then_inc(SB["v"], 1)
                act.wait_ge(SB["zs"], i + 1)
                act.activation(sbl[:], sbz[:], ACT.Abs)
                act.drain()
                act.activation(sbl[:], sbl[:], ACT.Exp, scale=-1.0)
                act.drain()
                act.activation(sbl[:], sbl[:], ACT.Ln, bias=1.0).then_inc(SB["ln"], 1)
                act.wait_ge(SB["u"], i + 1)
                act.activation(sbl[:], sbz[:], ACT.Exp).then_inc(SB["exp"], 1)
                act.wait_ge(SB["pv"], i + 1)
                act.activation(qkvu[:, bass.ds(i + 3 * HEADS, 1), :].rearrange("p e n -> p (e n)"), aux[:, 3, 0:SEQ],
                               ACT.Copy).then_inc(SB["out"], 1)
            act.wait_ge(SB["out"], HEADS)
            act.activation(ych[:], qkvu[:, 3 * HEADS:4 * HEADS, :], ACT.Copy).then_inc(yc_hi, 1)
            for g in range(2):
                high_parts(AT_POOL.past(g, g), 1)
                for ob in range(4):
                    if ob < 3:
                        act.wait_ge(block_done, 3 * (AT_POOL.g + g) + ob + 1)
                    else:
                        act.wait_ge(chunk_used, AT_POOL.n + g + 1)
                    if g == 0 and ob == 0:
                        act.wait_ge(yc_ready, 1)
                    act.activation(ybh[:, 4 * g + ob, :], acc[:, ob, 0:SEQ], ACT.Copy,
                                   scale=vec[:, VEC["pool_scale"] + 4 * g + ob:VEC["pool_scale"] + 4 * g + ob + 1])\
                        .then_inc(yb_hi, 1)
            with act.Fori(0, 4) as i:
                for b in range(3):
                    at = shifted(Turn(AT_MERGE, i, 3 * (CD + CH), 6), b * (CD + CH), 2 * b)
                    high_parts(at, CD)
                    act.wait_ge(bank_free, groups_behind(at, 4, 4 + 4))
                    act.activation(quad_a[:, :, 0:SEQ], quad_a[:, :, 0:SEQ], ACT.Sigmoid).then_inc(gate_out, 1)
                    high_parts(shifted(at, CD, 1), CH)
            for q in range(4):
                if q == 0:
                    act.wait_ge(m_in, 1)
                act.activation(mh[:, 4 * q:4 * q + 4, :], msum[:, 4 * q:4 * q + 4, :], ACT.Copy).then_inc(m_hi, 1)
            with act.Fori(0, 4) as i:
                residual(Turn(AT_OUT2, i, CD, 1), i * 4, "ffn2_g", slice(META, L), slice(0, SEQ), CD)
            inv_rms(rstd[:], aux[:, 3, 0:L], D, ss_sum, 4, rstd_ready)
            ffn(AT_FFN2, 11)
            with act.Fori(0, 2) as i:
                for k in range(2):
                    residual(shifted(Turn(AT_DOWN2, i, 2 * CF, 2), k * CF, k), i * 8 + 4 * k, None, slice(META, L), None,
                             CF)
            inv_rms(rstd[:], aux[:, 3, 0:L], D, ss_sum, 5, rstd_ready)

        @block.vector
        def _(dve):
            def low_parts(at, count):
                for j in range(AHEAD, AHEAD + count):
                    dve.wait_ge(hi_ready, chunks_behind(at, j + 1))
                    dve.tensor_tensor(wlo[:, slot_of(at, j), :], raw[:, slot_of(at, j), :],
                                      whi[:, slot_of(at, j), :].bitcast(F32), ALU.subtract).then_inc(lo_ready, 1)

            def wait_block(at, chunks, ob):
                if ob < 3:
                    dve.wait_ge(block_done, groups_behind(at, 3, ob + 1))
                else:
                    dve.wait_ge(chunk_used, chunks_behind(at, chunks))

            def times_rstd(at, chunks, dst, cols, scale=None, rows=P, blocks=4):
                scale = rstd if scale is None else scale
                n = cols.stop - cols.start
                for ob in range(blocks):
                    wait_block(at, chunks, ob if ob < blocks - 1 else 3)
                    dve.tensor_tensor(dst(ob), acc[0:rows, ob, 0:n], scale[0:rows, cols], ALU.mult)\
                        .then_inc(bank_free, 1)

            def add_squares(n, first):
                for ob in range(4):
                    if ob:
                        dve.drain()
                    last = dve.tensor_tensor(ss[:, L - n:L], ss[:, L - n:L], quad_b[:, ob, 0:n], ALU.add)
                return last

            def residual(at, b0, chunks, gain, cols, dst_cols, xh0, sq0):
                low_parts(at, chunks)
                n = cols.stop - cols.start
                for ob in range(4):
                    wait_block(at, chunks, ob)
                    hb = h[:, bass.ds(b0 + ob, 1), cols].rearrange("p e n -> p (e n)")
                    dve.tensor_tensor(hb, acc[:, ob, 0:n], hb, ALU.add).then_inc(bank_free, 1)
                for ob in range(4):
                    if gain is None:
                        break
                    dve.wait_ge(xh_ready, xh0(ob + 1))
                    dve.scalar_tensor_tensor(
                        xl[:, bass.ds(b0 + ob, 1), dst_cols].rearrange("p e n -> p (e n)"),
                        h[:, bass.ds(b0 + ob, 1), cols].rearrange("p e n -> p (e n)"),
                        vec[:, bass.ds(b0 + (VEC[gain] + ob), 1)],
                        xh[:, bass.ds(b0 + ob, 1), dst_cols].rearrange("p e n -> p (e n)").bitcast(F32),
                        ALU.mult, ALU.subtract)
                dve.wait_ge(sq_ready, sq0)
                add_squares(n, False).then_inc(x_ready, 1)

            def softmax_head(a, hd, bias, bias_dmas, bias_before, masked):
                s = a.s
                R, T, K = a.rows, a.tiles, a.keys
                dve.wait_ge(s["scores"], hd + 1)
                if bias is not None:
                    dve.wait_ge(bias_landed, hd * (16 * bias_dmas) + (bias_before + 16 * bias_dmas))
                    if masked:
                        dve.tensor_tensor(bias[0:R, 0:T, 0:K], bias[0:R, 0:T, 0:K], mask_s[0:R, 0:T, 0:K], ALU.add)
                        dve.drain()
                    dve.scalar_tensor_tensor(sx[0:R, 0:T, 0:K], aux[0:R, 0:T, 0:K], a.scale, bias[0:R, 0:T, 0:K],
                                             ALU.mult, ALU.add).then_inc(bias_free, 1)
                else:
                    dve.tensor_scalar(sx[0:R, 0:T, 0:K], aux[0:R, 0:T, 0:K], a.scale, None, ALU.mult)
                dve.drain()
                dve.tensor_reduce(small[0:R, 0, 0:T], sx[0:R, 0:T, 0:K], AX_X, ALU.max, negate=True)\
                    .then_inc(s["sx"], 1)
                dve.wait_ge(s["exp"], hd + 1)
                dve.reciprocal(small[0:R, 2, 0:T], small[0:R, 1, 0:T])
                dve.drain()
                for t in range(T):
                    last = dve.tensor_scalar(sx[0:R, t, 0:K], sx[0:R, t, 0:K], small[0:R, 2, t:t + 1], None, ALU.mult)
                last.then_inc(s["p"], 1)
                if len(a.kt) > 2:
                    dve.wait_ge(s["pt"], hd + 1)
                    _, _, kn_ = a.kt[2]
                    dve.tensor_copy(pt[0:kn_, 2, 0:a.nq], aux[0:kn_, 2, 0:a.nq]).then_inc(s["ptd"], 1)

            dve.memset(eps_s[:], EPS)
            dve.memset(ss[:], 0.0)
            dve.drain()
            dve.sem_inc(bank_free, 4)
            dve.sem_inc(eps_ready, 1)
            low_parts(At(-AHEAD, 0), AHEAD)
            dve.wait_ge(consts_landed, NCONST)
            for q in range(4):
                for k in range(4):
                    b = 4 * q + k
                    dve.wait_ge(xh_ready, b + 1)
                    dve.scalar_tensor_tensor(xl[:, b, :], h[:, b, :], vec[:, VEC["mix_g"] + b:VEC["mix_g"] + b + 1],
                                             xh[:, b, :].bitcast(F32), ALU.mult, ALU.subtract)
                dve.wait_ge(sq_ready, q + 1)
                add_squares(L, False).then_inc(x_ready, 1)
            dve.wait_ge(dist_sum, 1)
            dve.tensor_tensor(dist[:, 0:DISTS + 1], aux[0:HEADS, 0, 0:DISTS + 1], neg_s[:], ALU.add).then_inc(dist_ready, 1)
            dve.wait_ge(rstd_ready, 1)
            dve.memset(ss[:], 0.0)

            with dve.Fori(0, 6) as i:
                at = Turn(AT_QKV, i, CD, 1)
                low_parts(at, CD)
                times_rstd(at, CD, lambda ob: qkv[:, bass.ds(i * 4 + ob, 1), :].rearrange("p e n -> p (e n)"), slice(0, L))
            low_parts(AT_CQ, CD)
            times_rstd(AT_CQ, CD, lambda ob: quad_a[:, ob, :], slice(0, L))
            dve.wait_ge(lat_hi, 1)
            for k in range(CQB):
                last = dve.scalar_tensor_tensor(latl[:, k, :], quad_a[:, k, :], vec[:, VEC["cq_g"] + k:VEC["cq_g"] + k + 1],
                                                lath[:, k, :].bitcast(F32), ALU.mult, ALU.subtract)
            last.then_inc(lat_ready, 1)
            low_parts(AT_CKV, CD)
            for k in range(CKVB):
                wait_block(AT_CKV, CD, k)
                dve.tensor_tensor(quad_a[:, k, :], acc[:, k, 0:L], rstd[:], ALU.mult).then_inc(bank_free, 1)
            wait_block(AT_CKV, CD, 3)
            dve.tensor_tensor(kpe, acc[0:ROPE, 2, 0:L], rstd[0:ROPE, :], ALU.mult).then_inc(bank_free, 2)
            dve.wait_ge(lat_hi, 2)
            for k in range(CKVB):
                last = dve.scalar_tensor_tensor(latl[:, CQB + k, :], quad_a[:, k, :],
                                                vec[:, VEC["ckv_g"] + k:VEC["ckv_g"] + k + 1],
                                                lath[:, CQB + k, :].bitcast(F32), ALU.mult, ALU.subtract)
            last.then_inc(lat_ready, 1)
            dve.wait_ge(kpe_rot, 1)
            dve.tensor_tensor(kpe, aux[0:ROPE, 2, 0:L], sin_s, ALU.mult)
            dve.tensor_tensor(kpe_g, kpe_g, cos_s, ALU.mult)
            dve.drain()
            dve.tensor_tensor(kpe, kpe, kpe_g, ALU.add)
            dve.wait_ge(lat_rs, 1)
            done = 0
            for g, c in enumerate((2, 2, 1, 1)):
                at = AT_QUP.past(done, g)
                low_parts(at, c)
                if g < 2:
                    times_rstd(at, c, lambda ob: qnope[:, 4 * g + ob, :], slice(0, L), rs_a)
                else:
                    times_rstd(at, c, lambda ob: qrope[:, 4 * (g - 2) + ob, :], slice(0, L), rs_a, ROPE)
                done += c
            dve.wait_ge(lat_rs, 2)
            for g in range(4):
                at = AT_KVUP.past(g, g)
                low_parts(at, 1)
                times_rstd(at, 1, lambda ob: (knope if g < 2 else vmla)[:, 4 * (g % 2) + ob, :], slice(0, L), rs_b)

            with dve.Fori(0, HEADS) as i:
                dve.wait_ge(MLA.s["rs"], i + 1)
                dve.scalar_tensor_tensor(qn[:, 0:NQ], qnope[:, bass.ds(i, 1), Q0:L].rearrange("p e n -> p (e n)"),
                                         vec[:, VEC["q_nope_g"]:VEC["q_nope_g"] + 1], sq2[:, 0, Q0:L], ALU.mult, ALU.mult)
                dve.scalar_tensor_tensor(kn[:], knope[:, bass.ds(i, 1), :].rearrange("p e n -> p (e n)"),
                                         vec[:, VEC["k_nope_g"]:VEC["k_nope_g"] + 1], sq2[:, 1, :], ALU.mult, ALU.mult)
                dve.tensor_tensor(kr[:], kpe, sq2[0:ROPE, 1, :], ALU.mult)
                dve.tensor_tensor(qg[:], qg[:], cos_s, ALU.mult)
                dve.tensor_tensor(sqr[:], aux[0:ROPE, 2, 0:L], sin_s, ALU.mult)
                dve.drain()
                dve.tensor_tensor(sqr[:], sqr[:], qg[:], ALU.add)
                dve.drain()
                dve.tensor_tensor(qr[:, 0:NQ], sqr[:, Q0:L], sq2[0:ROPE, 0, Q0:L], ALU.mult).then_inc(MLA.s["qk"], 1)
                softmax_head(MLA, i, None, 0, 0, False)
            dve.wait_ge(mask_landed, 16)
            with dve.Fori(0, HEADS) as i:
                dve.wait_ge(NA.s["rs"], i + 1)
                dve.scalar_tensor_tensor(qn[:, 0:NQ], qkv[:, bass.ds(i, 1), Q0:L].rearrange("p e n -> p (e n)"),
                                         vec[:, VEC["na_q_g"]:VEC["na_q_g"] + 1], sq2[:, 0, Q0:L], ALU.mult, ALU.mult)
                dve.scalar_tensor_tensor(kn[:], qkv[:, bass.ds(i + HEADS, 1), :].rearrange("p e n -> p (e n)"),
                                         vec[:, VEC["na_k_g"]:VEC["na_k_g"] + 1], sq2[:, 1, :], ALU.mult, ALU.mult)\
                    .then_inc(NA.s["qk"], 1)
                softmax_head(NA, i, bias, 7, 0, True)

            for q in range(4):
                src, scale = (qkv, rs_a) if q < 2 else (qnope, rs_b)
                dve.wait_ge(mix_rs, 2)
                dve.drain()
                for k in range(4):
                    last = dve.scalar_tensor_tensor(quad_a[:, k, 0:NQ], src[:, 4 * (q % 2) + k, Q0:L],
                                                    vec[:, VEC["out_g"] + 4 * q + k:VEC["out_g"] + 4 * q + k + 1],
                                                    scale[:, 0:NQ], ALU.mult, ALU.mult)
                last.then_inc(mix_in, 1)
                dve.wait_ge(mix_hi, q + 1)
                dve.tensor_tensor(mixl[:, 4 * q:4 * q + 4, :], quad_a[:, :, 0:NQ],
                                  mixh[:, 4 * q:4 * q + 4, :].bitcast(F32), ALU.subtract).then_inc(mix_ready, 1)

            with dve.Fori(0, 4) as i:
                residual(Turn(AT_OUT, i, CD, 1), i * 4, CD, "ffn_g", slice(Q0, L), slice(Q0, L),
                         lambda b: i * 4 + (DB + b), i + 5)
            dve.wait_ge(rstd_ready, 2)
            dve.memset(ss[:], 0.0)
            dve.memset(quad_a[:, :, NQ:NQ + 1], 0.0)
            dve.drain()

            def ffn(start, turn0, conv):
                c0 = Q0 if conv else META
                nt = L - c0
                with dve.Fori(0, 11) as i:
                    at = Turn(start, i, 2 * CD, 2)
                    low_parts(at, CD)
                    times_rstd(at, CD, lambda ob: (quad_a if conv else quad_b)[:, ob, 0:nt], slice(c0, L))
                    if conv:
                        for tap in range(3):
                            dve.drain()
                            for ob in range(4):
                                w = vec[:, bass.ds(i * 4 + (VEC["conv_w"] + tap * FFB + ob), 1)]
                                src = quad_a[:, ob, 1 + tap:1 + tap + SEQ]
                                if tap == 0:
                                    last = dve.tensor_scalar(quad_b[:, ob, 0:SEQ], src, w,
                                                             vec[:, bass.ds(i * 4 + (VEC["conv_b"] + ob), 1)],
                                                             ALU.mult, ALU.add)
                                else:
                                    last = dve.scalar_tensor_tensor(quad_b[:, ob, 0:SEQ], src, w, quad_b[:, ob, 0:SEQ],
                                                                    ALU.mult, ALU.add)
                        last.then_inc(silu_in, 1)
                    else:
                        dve.drain()
                        dve.sem_inc(silu_in, 1)
                    at = shifted(at, CD, 1)
                    low_parts(at, CD)
                    dve.wait_ge(silu_out, i + (turn0 + 1))
                    dve.tensor_tensor(quad_b[:, :, 0:SEQ], quad_b[:, :, 0:SEQ],
                                      rstd[:, META:L].unsqueeze(1).to_broadcast([P, 4, SEQ]), ALU.mult)
                    dve.drain()
                    for ob in range(4):
                        wait_block(at, CD, ob)
                        dve.tensor_tensor(quad_a[:, ob, 0:SEQ], acc[:, ob, 0:SEQ], quad_b[:, ob, 0:SEQ], ALU.mult)\
                            .then_inc(bank_free, 1)
                    dve.wait_ge(act_hi, i + (turn0 + 1))
                    dve.tensor_tensor(actl[:, bass.ds(i * 4, 4), :], quad_a[:, :, 0:SEQ],
                                      acth[:, bass.ds(i * 4, 4), :].bitcast(F32), ALU.subtract).then_inc(act_ready, 1)

            ffn(AT_FFN, 0, True)
            with dve.Fori(0, 2) as i:
                for k in range(2):
                    residual(shifted(Turn(AT_DOWN, i, 2 * CF, 2), k * CF, k), i * 8 + 4 * k, CF, "mix2_g",
                             slice(META, L), slice(0, SEQ), lambda b: i * 8 + (2 * DB + 4 * k + b), i * 2 + (9 + k))
            dve.wait_ge(rstd_ready, 3)
            dve.memset(ss[:], 0.0)
            with dve.Fori(0, 14) as i:
                at = Turn(AT_IN2, i, CD, 1)
                low_parts(at, CD)
                times_rstd(at, CD, lambda ob: qkvu[:, bass.ds(i * 4 + ob, 1), :].rearrange("p e n -> p (e n)"),
                           slice(META, L))
            dve.sem_inc(ya_done, 1)
            with dve.Fori(0, HEADS) as i:
                softmax_head(MOBA, i, bias2, 2, 16 * 7 * HEADS, False)
                dve.wait_ge(MOBA.s["out"], i + 1)
                dve.tensor_tensor(yal[:, bass.ds(i, 1), :].rearrange("p e n -> p (e n)"), aux[:, 3, 0:SEQ],
                                  yah[:, bass.ds(i, 1), :].rearrange("p e n -> p (e n)").bitcast(F32), ALU.subtract)\
                    .then_inc(ya_done, 1)
            dve.wait_ge(tables_landed, 48)
            dve.memset(quad_a[:, :, 0:META], 0.0)
            dve.memset(quad_b[:, :, 0:META], 0.0)
            for g, w in enumerate(WINDOWS):
                u = qkvu[:, 6 * HEADS + 2 * g:6 * HEADS + 2 * g + 2, :]
                dve.drain()
                dve.tensor_copy(quad_b[:, 0:2, META:L], u)
                src, dst = quad_b[:, 0:2], quad_b[:, 2:4]
                step = 1
                while step < w:
                    dve.drain()
                    dve.tensor_tensor(dst[:, :, META:L], src[:, :, META:L], src[:, :, META - step:L - step], ALU.add)
                    src, dst = dst, src
                    step *= 2
                dve.drain()
                dve.tensor_tensor(quad_a[:, 2:4, 0:META], src[:, :, META:2 * META],
                                  invc[:, g, :].unsqueeze(1).to_broadcast([P, 2, META]), ALU.mult)
                dve.scalar_tensor_tensor(quad_a[:, 2:4, META:SEQ], src[:, :, 2 * META:L], 1.0 / w, u[:, :, META:SEQ],
                                         ALU.mult, ALU.subtract)
                dve.drain()
                dve.tensor_tensor(quad_a[:, 2:4, 0:META], quad_a[:, 2:4, 0:META], u[:, :, 0:META], ALU.subtract)\
                    .then_inc(pool_in, 1)
                dve.wait_ge(pool_hi, g + 1)
                dve.tensor_tensor(pl[:, 2 * g:2 * g + 2, :], quad_a[:, 2:4, 0:SEQ], ph[:, 2 * g:2 * g + 2, :].bitcast(F32),
                                  ALU.subtract).then_inc(pool_ready, 1)
            with dve.Fori(0, HEADS) as i:
                dve.wait_ge(SB["z"], i + 1)
                dve.tensor_scalar(sbz[:], aux[:, 0, 0:SBN], float(P) ** -0.5, None, ALU.mult).then_inc(SB["zs"], 1)
                dve.wait_ge(SB["ln"], i + 1)
                dve.scalar_tensor_tensor(sbs[:], sbz[:], 0.0, sbl[:], ALU.max, ALU.add)
                dve.drain()
                for c in (0, 2 * P):
                    last = dve.tensor_tensor(sbs[:, c:c + P], sbs[:, c:c + P], triu_s[:], ALU.mult)
                last.then_inc(SB["sp"], 1)
                dve.scalar_tensor_tensor(sbz[:], sbz[:], 0.0, sbl[:], ALU.min, ALU.subtract)
                dve.drain()
                dve.wait_ge(SB["cum"], i + 1)
                dve.tensor_tensor(sbz[:], sbz[:], aux[:, 2, 0:SBN], ALU.subtract).then_inc(SB["u"], 1)
                dve.wait_ge(SB["exp"], i + 1)
                for c in (0, 2 * P):
                    last = dve.tensor_tensor(sbl[:, c:c + P], sbl[:, c:c + P], triu_s[:], ALU.mult)
                last.then_inc(SB["a"], 1)
            dve.wait_ge(yc_hi, 1)
            dve.tensor_tensor(ycl[:], qkvu[:, 3 * HEADS:4 * HEADS, :], ych[:].bitcast(F32), ALU.subtract).then_inc(yc_ready, 1)
            for g in range(2):
                low_parts(AT_POOL.past(g, g), 1)
                for ob in range(4):
                    dve.wait_ge(yb_hi, 4 * g + ob + 1)
                    dve.scalar_tensor_tensor(ybl[:, 4 * g + ob, :], acc[:, ob, 0:SEQ],
                                             vec[:, VEC["pool_scale"] + 4 * g + ob:VEC["pool_scale"] + 4 * g + ob + 1],
                                             ybh[:, 4 * g + ob, :].bitcast(F32), ALU.mult, ALU.subtract)\
                        .then_inc(bank_free, 1)
            with dve.Fori(0, 4) as i:
                for b in range(3):
                    at = shifted(Turn(AT_MERGE, i, 3 * (CD + CH), 6), b * (CD + CH), 2 * b)
                    low_parts(at, CD)
                    times_rstd(at, CD, lambda ob: quad_a[:, ob, 0:SEQ], slice(META, L))
                    at = shifted(at, CD, 1)
                    low_parts(at, CH)
                    dve.wait_ge(gate_out, i * 3 + (b + 1))
                    for ob in range(4):
                        m = msum[:, bass.ds(i * 4 + ob, 1), :].rearrange("p e n -> p (e n)")
                        wait_block(at, CH, ob)
                        dve.tensor_tensor(m if b == 0 else quad_b[:, ob, 0:SEQ], acc[:, ob, 0:SEQ], quad_a[:, ob, 0:SEQ],
                                          ALU.mult).then_inc(bank_free, 1)
                    dve.drain()
                    if b:
                        last = dve.tensor_tensor(msum[:, bass.ds(i * 4, 4), :], msum[:, bass.ds(i * 4, 4), :],
                                                 quad_b[:, :, 0:SEQ], ALU.add)
            dve.drain()
            dve.sem_inc(m_in, 1)
            for q in range(4):
                dve.wait_ge(m_hi, q + 1)
                dve.tensor_tensor(ml[:, 4 * q:4 * q + 4, :], msum[:, 4 * q:4 * q + 4, :],
                                  mh[:, 4 * q:4 * q + 4, :].bitcast(F32), ALU.subtract).then_inc(m_ready, 1)
            with dve.Fori(0, 4) as i:
                residual(Turn(AT_OUT2, i, CD, 1), i * 4, CD, "ffn2_g", slice(META, L), slice(0, SEQ),
                         lambda b: i * 4 + (3 * DB + b), i + 13)
            dve.wait_ge(rstd_ready, 4)
            dve.memset(ss[:], 0.0)
            ffn(AT_FFN2, 11, False)
            with dve.Fori(0, 2) as i:
                for k in range(2):
                    residual(shifted(Turn(AT_DOWN2, i, 2 * CF, 2), k * CF, k), i * 8 + 4 * k, CF, None, slice(META, L),
                             None, None, i * 2 + (17 + k))
            dve.wait_ge(rstd_ready, 5)
            for b in range(DB):
                last = dve.scalar_tensor_tensor(h[:, b, META:L], h[:, b, META:L],
                                                vec[:, VEC["final_g"] + b:VEC["final_g"] + b + 1], rstd[:, META:L],
                                                ALU.mult, ALU.mult)
                if b % 4 == 3:
                    last.then_inc(out_ready, 1)

        @block.tensor
        def _(pe):
            def group(at, chunks, x_hi, x_lo, n, blocks=4, width=P, row=GC, per_chunk=2, kt0=None):
                for j in range(chunks):
                    slot = slot_of(at, j)
                    pe.wait_ge(lo_ready, chunks_behind(at, j + 1))
                    for ob in range(blocks):
                        if j == 0:
                            pe.wait_ge(bank_free, groups_behind(at, 4, ob + 1))
                        w = P if blocks == 4 or ob < blocks - 1 else ROPE
                        w = width if blocks == 4 else w
                        dst = acc[0:w, ob, 0:n]
                        for t in range(per_chunk):
                            c = t * row + ob * width
                            hi, lo = whi[:, slot, c:c + w], wlo[:, slot, c:c + w]
                            kt = j * per_chunk + t
                            first, final = kt == 0, kt == chunks * per_chunk - 1
                            pe.matmul(dst, hi, x_hi(kt), start=first, stop=False)
                            pe.matmul(dst, hi, x_lo(kt), start=False, stop=False)
                            last = pe.matmul(dst, lo, x_hi(kt), start=False, stop=final)
                        if j == chunks - 1 and ob < blocks - 1:
                            last.then_inc(block_done, 1 if ob < blocks - 2 else 5 - blocks)
                    last.then_inc(chunk_used, 1)

            def token_sums(kind_wait, n_wait, cols):
                pe.wait_ge(kind_wait, n_wait)
                pe.matmul(aux[:, 3, 0:L], ones_s[:], ss[:], start=True, stop=True).then_inc(ss_sum, 1)

            def softmax_head(a, hd, scores):
                s = a.s
                pe.wait_ge(s["qk"], hd + 1)
                scores()
                pe.wait_ge(s["p"], hd + 1)
                for t in range(a.tiles):
                    for kt, k, kn_ in a.kt:
                        last = pe.transpose(aux[0:kn_, kt, t * a.rows:(t + 1) * a.rows], sx[0:a.rows, t, k:k + kn_],
                                            ident_s[0:a.rows, 0:a.rows])
                last.then_inc(s["pt"], 1)
                pe.wait_ge(s["ptc"], hd + 1)
                if len(a.kt) > 2:
                    pe.wait_ge(s["ptd"], hd + 1)
                for kt, k, kn_ in a.kt:
                    last = pe.matmul(aux[:, 3, 0:a.nq], vt[0:kn_, kt, :], pt[0:kn_, kt, 0:a.nq], start=kt == 0,
                                     stop=kt == len(a.kt) - 1)
                last.then_inc(s["pv"], 1)

            def value_transposes(src, tiles):
                for kt, k, kn_ in tiles:
                    last = pe.transpose(aux[0:kn_, 3, kt * P:kt * P + P], src[:, k:k + kn_], ident_s[:])
                return last

            def x1(t):
                return lambda kt: t[:, kt, :]

            pe.wait_ge(consts_landed, NCONST)
            pe.wait_ge(dist_landed, 48)
            pe.matmul(aux[0:HEADS, 0, 0:DISTS + 1], relT_s[:], onehot_s[:], start=True, stop=True).then_inc(dist_sum, 1)
            token_sums(x_ready, 4, L)
            with pe.Fori(0, 6) as i:
                group(Turn(AT_QKV, i, CD, 1), CD, x1(xh), x1(xl), L)
            group(AT_CQ, CD, x1(xh), x1(xl), L)
            for k in range(CQB):
                if k == 0:
                    pe.wait_ge(lat_hi, 1)
                    pe.wait_ge(rstd_ready, 1)
                last = pe.matmul(aux[:, 3, 0:L], ones_s[:], quad_b[:, k, :], start=k == 0, stop=k == CQB - 1)
            last.then_inc(lat_sum, 1)
            group(AT_CKV, CD, x1(xh), x1(xl), L, blocks=3)
            pe.wait_ge(lat_hi, 2)
            pe.wait_ge(lat_rs, 1)
            for k in range(CKVB):
                last = pe.matmul(aux[:, 3, 0:L], ones_s[:], quad_b[:, k, :], start=k == 0, stop=k == CKVB - 1)
            last.then_inc(lat_sum, 1)
            pe.matmul(aux[0:ROPE, 2, 0:L], rot_s[:], kpe_g, start=True, stop=True).then_inc(kpe_rot, 1)
            pe.wait_ge(lat_ready, 1)
            group(AT_QUP, 2, x1(lath), x1(latl), L)
            group(AT_QUP.past(2, 1), 2, x1(lath), x1(latl), L)
            for g in range(2):
                group(AT_QUP.past(4 + g, 2 + g), 1, x1(lath), x1(latl), L, width=ROPE, row=4 * ROPE, per_chunk=4)
            pe.wait_ge(lat_ready, 2)
            for g in range(4):
                group(AT_KVUP.past(g, g), 1, lambda kt: lath[:, CQB + kt, :], lambda kt: latl[:, CQB + kt, :], L)

            with pe.Fori(0, HEADS) as i:
                pe.wait_ge(MLA.s["sq"], i + 1)
                for k in range(2):
                    pe.matmul(aux[:, k, 0:L], ones_s[:], sq2[:, k, :], start=True, stop=False)
                    pe.matmul(aux[:, k, 0:L], ones_s[0:ROPE, :], sqr[:] if k == 0 else kpe_sq, start=False, stop=True)
                pe.matmul(aux[0:ROPE, 2, 0:L], rot_s[:], qg[:], start=True, stop=True)
                value_transposes(vc, MLA.kt).then_inc(MLA.s["sums"], 1)

                def scores():
                    for t in range(QT):
                        dst = aux[0:QR, t, 0:L]
                        pe.matmul(dst, qn[:, t * QR:(t + 1) * QR], kn[:], start=True, stop=False)
                        last = pe.matmul(dst, qr[:, t * QR:(t + 1) * QR], kr[:], start=False, stop=True)
                    last.then_inc(MLA.s["scores"], 1)
                softmax_head(MLA, i, scores)
            with pe.Fori(0, HEADS) as i:
                pe.wait_ge(NA.s["sq"], i + 1)
                for k in range(2):
                    pe.matmul(aux[:, k, 0:L], ones_s[:], sq2[:, k, :], start=True, stop=True)
                value_transposes(vc, NA.kt).then_inc(NA.s["sums"], 1)

                def scores():
                    for t in range(QT):
                        last = pe.matmul(aux[0:QR, t, 0:L], qn[:, t * QR:(t + 1) * QR], kn[:], start=True, stop=True)
                    last.then_inc(NA.s["scores"], 1)
                softmax_head(NA, i, scores)

            for q in range(4):
                pe.wait_ge(mix_sq, q + 1)
                for k in range(4):
                    last = pe.matmul(aux[:, q // 2, 0:NQ], ones_s[:], quad_b[:, k, 0:NQ], start=q % 2 == 0 and k == 0,
                                     stop=q % 2 == 1 and k == 3)
                last.then_inc(mix_sum, 1)
            pe.wait_ge(mix_ready, 4)
            with pe.Fori(0, 4) as i:
                group(Turn(AT_OUT, i, CD, 1), CD, x1(mixh), x1(mixl), NQ)
            token_sums(x_ready, 8, L)

            def ffn(start, c0, c1, n):
                with pe.Fori(0, 11) as i:
                    at = Turn(start, i, 2 * CD, 2)
                    group(at, CD, lambda kt: xh[:, kt, c0:c0 + n], lambda kt: xl[:, kt, c0:c0 + n], n)
                    group(shifted(at, CD, 1), CD, lambda kt: xh[:, kt, c1:c1 + SEQ], lambda kt: xl[:, kt, c1:c1 + SEQ],
                          SEQ)

            def down(start):
                with pe.Fori(0, 2) as i:
                    for k in range(2):
                        group(shifted(Turn(start, i, 2 * CF, 2), k * CF, k), CF, x1(acth), x1(actl), SEQ)

            def x2(t):
                return lambda kt: t[:, kt, 0:SEQ]

            ffn(AT_FFN, Q0, META, NQ)
            pe.wait_ge(act_ready, 11)
            down(AT_DOWN)
            token_sums(x_ready, 12, L)
            with pe.Fori(0, 14) as i:
                group(Turn(AT_IN2, i, CD, 1), CD, x2(xh), x2(xl), SEQ)
            with pe.Fori(0, HEADS) as i:
                def scores():
                    for t in range(2):
                        if t == 0:
                            pe.wait_ge(ya_done, i + 1)
                        pe.matmul(aux[:, t, 0:SEQ], mq[:, 0, t * P:(t + 1) * P], mq[:, 1, :], start=True, stop=True)
                    value_transposes(mq[:, 2, :], MOBA.kt).then_inc(MOBA.s["scores"], 1)
                softmax_head(MOBA, i, scores)
            pe.wait_ge(ya_done, HEADS + 1)
            pe.wait_ge(tables_landed, 48)
            with pe.Fori(0, HEADS) as i:
                pe.wait_ge(SB["copy"], i + 1)
                pe.matmul(aux[:, 0, 0:SEQ], sbq[:, 1, 0:P], sbq[:, 0, :], start=True, stop=True)
                pe.matmul(aux[:, 0, SEQ:SBN], sbq[:, 1, P:SEQ], sbq[:, 0, P:SEQ], start=True, stop=True)
                for t in range(2):
                    last = pe.transpose(aux[:, 1, t * P:(t + 1) * P], sbq[:, 2, t * P:(t + 1) * P], ident_s[:])
                last.then_inc(SB["z"], 1)
                pe.wait_ge(SB["sp"], i + 1)
                pe.matmul(aux[:, 2, 0:SEQ], tril_s[:], sbs[:, 0:SEQ], start=True, stop=False)
                pe.matmul(aux[:, 2, P:SEQ], ones_s[:], sbs[:, SEQ:SBN], start=False, stop=True)
                pe.matmul(aux[:, 2, SEQ:SBN], tril_s[:], sbs[:, SEQ:SBN], start=True, stop=True).then_inc(SB["cum"], 1)
                pe.wait_ge(SB["a"], i + 1)
                pe.wait_ge(SB["v"], i + 1)
                pe.matmul(aux[:, 3, 0:SEQ], sbv[:, 0, :], sbl[:, 0:SEQ], start=True, stop=False)
                pe.matmul(aux[:, 3, P:SEQ], sbv[:, 1, :], sbl[:, SEQ:SBN], start=False, stop=True).then_inc(SB["pv"], 1)
            pe.wait_ge(pool_ready, 4)
            for g in range(2):
                at = AT_POOL.past(g, g)
                slot = slot_of(at, 0)
                pe.wait_ge(lo_ready, at.n + 1)
                for ob in range(4):
                    pe.wait_ge(bank_free, 4 * at.g + ob + 1)
                    for t in range(2):
                        c = (ob // 2) * 512 + t * 256 + (ob % 2) * P
                        b = 4 * g + 2 * (ob // 2) + t
                        hi, lo = whi[:, slot, c:c + P], wlo[:, slot, c:c + P]
                        pe.matmul(acc[:, ob, 0:SEQ], hi, ph[:, b, :], start=t == 0, stop=False)
                        pe.matmul(acc[:, ob, 0:SEQ], hi, pl[:, b, :], start=False, stop=False)
                        last = pe.matmul(acc[:, ob, 0:SEQ], lo, ph[:, b, :], start=False, stop=t == 1)
                    if ob < 3:
                        last.then_inc(block_done, 1)
                last.then_inc(chunk_used, 1)
            with pe.Fori(0, 4) as i:
                for b, (yh, yl) in enumerate(((yah, yal), (ybh, ybl), (ych, ycl))):
                    at = shifted(Turn(AT_MERGE, i, 3 * (CD + CH), 6), b * (CD + CH), 2 * b)
                    group(at, CD, x2(xh), x2(xl), SEQ)
                    group(shifted(at, CD, 1), CH, x1(yh), x1(yl), SEQ)
            pe.wait_ge(m_ready, 4)
            with pe.Fori(0, 4) as i:
                group(Turn(AT_OUT2, i, CD, 1), CD, x1(mh), x1(ml), SEQ)
            token_sums(x_ready, 16, L)
            ffn(AT_FFN2, 0, 0, SEQ)
            pe.wait_ge(act_ready, 22)
            down(AT_DOWN2)
            token_sums(x_ready, 20, L)


def _blocks(a, n):
    return np.ascontiguousarray(np.asarray(a).reshape(n, P).T)


def _chunks(w, c0, c1, rows=2, width=GC):
    part = w[:, c0:c1]
    if c1 - c0 < width:
        part = np.concatenate([part, np.zeros((w.shape[0], width - (c1 - c0)), w.dtype)], axis=1)
    n = w.shape[0] // (rows * P)
    return part.reshape(n, rows, P, width).transpose(0, 2, 1, 3).reshape(n, P, rows * width)


def _layout(inputs):
    f = {k: np.asarray(v) for k, v in inputs.items()}
    one = {k: f[k][0] for k in ("w_in", "w_q_up", "w_kv_up", "w_out", "w_gate", "w_up", "w_down", "w_in_2", "w_pool_2",
                                "w_br_a_2", "w_br_b_2", "w_br_c_2", "w_out_2", "w_gate_2", "w_up_2", "w_down_2")}
    stream = []

    def groups(w, lo=0, hi=None):
        for c in range(lo, w.shape[1] if hi is None else hi, GC):
            stream.append(_chunks(w, c, c + GC))

    w_in = one["w_in"]
    q_cols = 3 * HEADS * P
    groups(w_in, 0, q_cols + CQB * P)
    stream.append(_chunks(w_in, q_cols + CQB * P, w_in.shape[1]))
    q_up = one["w_q_up"].reshape(-1, HEADS, MLA_QK)
    groups(q_up[:, :, :P].reshape(-1, HEADS * P))
    rope_cols = q_up[:, :, P:].reshape(-1, HEADS * ROPE)
    for c in range(0, HEADS * ROPE, 4 * ROPE):
        stream.append(_chunks(rope_cols, c, c + 4 * ROPE, rows=4, width=4 * ROPE))
    kv_up = one["w_kv_up"].reshape(-1, HEADS, 2, P)
    groups(kv_up[:, :, 0].reshape(-1, HEADS * P))
    groups(kv_up[:, :, 1].reshape(-1, HEADS * P))
    groups(one["w_out"])
    for c in range(0, FF, GC):
        groups(one["w_gate"], c, c + GC)
        groups(one["w_up"], c, c + GC)
    groups(one["w_down"])
    w2 = one["w_in_2"]
    groups(w2, 0, q_cols)
    groups(w2, q_cols + HEADS * P, 2 * q_cols + HEADS * P)
    groups(w2, q_cols, q_cols + HEADS * P)
    gates = 2 * q_cols + HEADS * P
    wp = one["w_pool_2"].reshape(2, 2, 2, P, 2 * P)
    stream.append(wp.transpose(0, 3, 1, 2, 4).reshape(2, P, CE))
    for c in range(0, D, GC):
        for b, name in enumerate(("w_br_a_2", "w_br_b_2", "w_br_c_2")):
            groups(w2, gates + b * D + c, gates + b * D + c + GC)
            groups(one[name], c, c + GC)
    groups(one["w_out_2"])
    for c in range(0, FF, GC):
        groups(one["w_gate_2"], c, c + GC)
        groups(one["w_up_2"], c, c + GC)
    groups(one["w_down_2"])
    stream.append(np.zeros((RING, P, CE), np.float32))
    wts = np.concatenate(stream)

    def column(a, n=P):
        c = np.zeros((P, 1), np.float32)
        c[:n, 0] = a
        return c

    cols = dict(
        mix_g=_blocks(f["mix_norm_g"], DB), ffn_g=_blocks(f["ffn_norm_g"], DB),
        conv_w=_blocks(f["conv_w"], 3 * FFB), conv_b=_blocks(f["conv_b"], FFB),
        cq_g=_blocks(f["mla_cq_g"], CQB), ckv_g=_blocks(f["mla_ckv_g"], CKVB),
        na_q_g=column(f["na_q_g"][0]), na_k_g=column(f["na_k_g"][0]),
        q_nope_g=column(f["mla_q_g"][0, :P]), q_rope_g=column(f["mla_q_g"][0, P:], ROPE),
        k_nope_g=column(f["mla_k_g"][0, :P]), k_rope_g=column(f["mla_k_g"][0, P:], ROPE),
        out_g=np.concatenate([_blocks(f["na_out_g"], HEADS), _blocks(f["mla_out_g"], HEADS)], axis=1),
        mix2_g=_blocks(f["norm_mix_2"], DB), ffn2_g=_blocks(f["norm_ffn_2"], DB),
        final_g=_blocks(f["norm_final_2"], DB), pool_scale=_blocks(f["pool_scale_2"], HEADS))
    assert all(cols[k].shape[1] == n for k, n in VEC_SIZES.items())
    vecs = np.concatenate([cols[k] for k in VEC_SIZES], axis=1)

    tokens = np.concatenate([f["meta_tokens"], f["x"][0]], axis=0)
    hT = tokens.T.reshape(DB, P, L).transpose(1, 0, 2)
    rpb = f["na_rpb"][0]
    rows = np.zeros((HEADS, RPR, RPW), rpb.dtype)
    lo = GRID - 1 - (rpb.shape[2] // 2)
    rows[:, :, lo:lo + rpb.shape[2]] = rpb
    rp = np.stack([rows[:, :, GRID - 1 - c:2 * GRID - 1 - c] for c in range(GRID)])
    return dict(hT=hT, wts=wts, vecs=vecs, rp=rp, meta_b=f["na_meta_bias"][0], relT=f["rel_bias_2"].T, **_constants())


def _constants():
    f4 = np.float32
    i = np.arange(P)
    half = ROPE // 2
    rot = np.zeros((ROPE, ROPE), f4)
    rot[np.arange(half) + half, np.arange(half)] = -1
    rot[np.arange(half), np.arange(half) + half] = 1
    inv = (f4(10000.0) ** (-np.arange(0, ROPE, 2, dtype=f4) / f4(ROPE))).astype(f4)
    ang = np.concatenate([inv, inv])[:, None] * np.arange(L, dtype=f4)[None, :]
    c = np.arange(GRID)
    start = np.clip(c - 8, 0, GRID - 16)
    seen = (c[None] >= start[:, None]) & (c[None] < start[:, None] + 16)
    mask = np.zeros((NQ, L), f4)
    mask[2:, META:] = np.where(np.tile(seen, (ROWS, ROWS)), 0.0, NEG)
    mask[:2, META:] = NEG
    dist = SEQ - 1 - np.arange(DISTS)
    nf = np.maximum(dist, 1).astype(f4)
    large = 16 + (np.log(nf / f4(16)) / f4(np.log(2048 / 16)) * f4(16)).astype(np.int32)
    bucket = np.where(dist < 16, np.maximum(dist, 0), np.minimum(large, BUCKETS - 1))
    onehot = np.zeros((BUCKETS, DISTS + 1), f4)
    causal = dist >= 0
    onehot[bucket[causal], np.arange(DISTS)[causal]] = 1
    neg = np.zeros((HEADS, DISTS + 1), f4)
    neg[:, :DISTS][:, ~causal] = NEG
    count = np.minimum(np.arange(META)[None] + 1, np.array(WINDOWS)[:, None]).astype(f4)
    return dict(ident=np.eye(P, dtype=f4), ones=np.ones((P, P), f4), tril=(i[:, None] > i[None]).astype(f4),
                triu=(i[:, None] < i[None]).astype(f4), rot=rot, cos=np.cos(ang).astype(f4), sin=np.sin(ang).astype(f4),
                na_mask=mask.reshape(QT, QR, L).transpose(1, 0, 2), onehot=onehot, neg=neg,
                inv_count=np.broadcast_to(f4(1) / count, (P, len(WINDOWS), META)))


_ARGS = ("hT", "wts", "vecs", "ident", "ones", "tril", "triu", "rot", "cos", "sin", "rp", "meta_b", "na_mask", "relT",
         "onehot", "neg", "inv_count")


def kernel(**inputs):
    import concourse.bacc as bacc
    from concourse.bass_utils import run_bass_kernel_spmd

    nc = bacc.Bacc("TRN2", target_bir_lowering=False, num_devices=1)
    given = _layout(inputs)
    arrays, args = {}, []
    for name in _ARGS:
        a = np.ascontiguousarray(given[name])
        arrays[f"in_{name}"] = a
        args.append(nc.dram_tensor(f"in_{name}", a.shape, F32, kind="ExternalInput").ap())
    out = nc.dram_tensor("out_T", (P, DB, SEQ), F32, kind="ExternalOutput").ap()
    build(nc, *args, out)
    r = run_bass_kernel_spmd(nc, [arrays], core_ids=[0])
    got = np.asarray(r.results[0]["out_T"])
    return np.ascontiguousarray(got.transpose(2, 1, 0).reshape(1, SEQ, D))
```

```python
from contextlib import ExitStack

import numpy as np

import concourse.bass as bass
from concourse import mybir

F32 = mybir.dt.float32
F32R = mybir.dt.float32r
ACT = mybir.ActivationFunctionType
ALU = mybir.AluOpType
AX_X = mybir.AxisListType.X

P = 128
D = 2048
DB = D // P
META = 16
SEQ = 256
L = META + SEQ
Q0 = META - 2
NQ = L - Q0
QT = 3
QR = NQ // QT
HEADS = 8
EPS = 1e-6
NEG = -1e30
FF = 5632
FFB = FF // P
GRID = 64
ROWS = SEQ // GRID
RPR, RPW = 15, 2 * GRID - 1
ROPE = 64
CQB, CKVB = 4, 2
MLA_QK = 192
WINDOWS = (2, 4, 8, 16)
DISTS = 2 * SEQ - 1
BUCKETS = 32

GC = 512
CE = 1024
RING = 4
AHEAD = 2
CD = DB // 2
CF = FFB // 2
CH = HEADS // 2

VEC_SIZES = dict(mix_g=DB, ffn_g=DB, conv_w=3 * FFB, conv_b=FFB, cq_g=CQB, ckv_g=CKVB, na_q_g=1,
                 na_k_g=1, q_nope_g=1, q_rope_g=1, k_nope_g=1, k_rope_g=1, out_g=DB, mix2_g=DB,
                 ffn2_g=DB, final_g=DB, pool_scale=HEADS)
VEC = {name: sum(list(VEC_SIZES.values())[:i]) for i, name in enumerate(VEC_SIZES)}
NVEC = sum(VEC_SIZES.values())


class At:

    def __init__(self, n=0, g=0):
        self.n, self.g = n, g

    def past(self, chunks, groups):
        return At(self.n + chunks, self.g + groups)


class Turn:

    def __init__(self, at, i, chunks, groups):
        assert chunks % RING == 0
        self.first, self.i, self.chunks, self.groups = at, i, chunks, groups


def chunks_behind(at, j=0):
    return at.n + j if isinstance(at, At) else at.i * at.chunks + (at.first.n + j)


def groups_behind(at, per, j=0):
    return at.g * per + j if isinstance(at, At) else at.i * (at.groups * per) + (at.first.g * per + j)


def shifted(at, chunks, groups):
    if isinstance(at, At):
        return at.past(chunks, groups)
    return Turn(at.first.past(chunks, groups), at.i, at.chunks, at.groups)


def slot_of(at, j):
    return (at.n + j if isinstance(at, At) else at.first.n + j) % RING


def loads_of_slot(at, j):
    if isinstance(at, At):
        return (at.n + j) // RING + 1
    return at.i * (at.chunks // RING) + ((at.first.n + j) // RING + 1)


def build(nc, hT, wts, vecs, ident, ones, tril, triu, rot, cos_sin, rp, meta_b, na_mask, relT, onehot,
          neg, inv_count, out):
    NCH = wts.shape[0]
    dist_dram = nc.dram_tensor("distances", (P, HEADS, DISTS + 1), F32, kind="Internal").ap()
    with ExitStack() as ctx:
        def sb(name, shape, dt=F32):
            return ctx.enter_context(nc.sbuf_tensor(name, shape, dt))

        def sem(name):
            return ctx.enter_context(nc.semaphore(name))

        h = sb("h", [P, DB, L])
        xh = sb("xh", [P, DB, L], F32R)
        xl = sb("xl", [P, DB, L], F32R)
        raw = sb("raw", [P, RING, CE])
        whi = sb("whi", [P, RING, CE], F32R)
        wlo = sb("wlo", [P, RING, CE], F32R)
        vec = sb("vec", [P, NVEC])
        ident_s = sb("ident_s", [P, P])
        ones_s = sb("ones_s", [P, P])
        rstd = sb("rstd", [P, L])
        rs_a = sb("rs_a", [P, L])
        rs_b = sb("rs_b", [P, L])
        ss = sb("ss", [P, L])
        small = sb("small", [P, 4, 3])
        quad_a = sb("quad_a", [P, 4, L])
        quad_b = sb("quad_b", [P, 4, L])
        eps_s = sb("eps_s", [P, 1])
        rot_s = sb("rot_s", [ROPE, ROPE])
        tab = sb("tab", [ROPE, 4, L])
        BIG = 90496
        arena = (nc.sbuf_usable_end - BIG) // 32 * 32
        assert nc.sbuf_base <= arena

        def at(name, offset, shape, dt=F32):
            return nc.alloc_sbuf_tensor_at(name, shape, dt, offset=arena + offset)

        qkv = at("qkv", 0, [P, 3 * HEADS, L])
        mixah = at("mixah", 0, [P, HEADS, L], F32R)
        mixal = at("mixal", 8704, [P, HEADS, L], F32R)
        lath = at("lath", 26112, [P, 6, L], F32R)
        latl = at("latl", 32640, [P, 6, L], F32R)
        qrope = at("qrope", 39168, [ROPE, HEADS, L])
        knope = at("knope", 47872, [P, HEADS, L])
        vmla = at("vmla", 56576, [P, HEADS, L])
        qnope = at("qnope", 65280, [P, HEADS, L])
        mixbh = at("mixbh", 65280, [P, HEADS, L], F32R)
        mixbl = at("mixbl", 47872, [P, HEADS, L], F32R)
        T0 = 73984
        sq2 = at("sq2", T0, [P, 2, L])
        qn = at("qn", T0 + 2176, [P, L])
        kn = at("kn", T0 + 3264, [P, L])
        qr = at("qr", T0 + 4352, [ROPE, L])
        kr = at("kr", T0 + 5440, [ROPE, L])
        vc = at("vc", T0 + 6528, [P, L])
        vt = at("vt", T0 + 7616, [P, 3, P])
        sx = at("sx", T0 + 9152, [P, 3, L])
        pt = at("pt", T0 + 12416, [P, 3, NQ])
        sqr = at("sqr", T0 + 12416, [ROPE, L])
        qg = at("qg", T0 + 13504, [ROPE, L])
        osq = at("osq", T0 + 14592, [P, NQ])
        mq = at("mq", T0, [P, 3, SEQ])
        dist = quad_a[0:HEADS].rearrange("p e n -> p (e n)")[:, 0:DISTS + 1]
        onehot_s = at("onehot_s", T0 + 2048, [BUCKETS, DISTS + 1])
        neg_s = at("neg_s", T0 + 4096, [HEADS, DISTS + 1])
        relT_s = at("relT_s", T0 + 6144, [BUCKETS, HEADS])
        bias = at("bias", 26112, [P, 3, L])
        mask_s = at("mask_s", 29376, [P, 3, L])
        bias2 = at("bias2", T0 + 4352, [P, 2, SEQ])
        acth = at("acth", 0, [P, FFB, SEQ], F32R)
        actl = at("actl", FFB * SEQ * 4, [P, FFB, SEQ], F32R)
        qkvu = at("qkvu", 0, [P, 56, SEQ])
        yah = at("yah", 57344, [P, HEADS, SEQ], F32R)
        yal = at("yal", 65536, [P, HEADS, SEQ], F32R)
        ph = at("ph", 0, [P, HEADS, SEQ], F32R)
        pl = at("pl", 8192, [P, HEADS, SEQ], F32R)
        pool_a = at("pool_a", 6 * 1024, [P, 2, SEQ])
        pool_b = at("pool_b", 14 * 1024, [P, 2, SEQ])
        SBN = 3 * P
        sbz = at("sbz", 16384, [P, SBN])
        sbl = at("sbl", 17920, [P, SBN])
        sbs = at("sbs", 19456, [P, SBN])
        sbv = at("sbv", 20992, [P, 2, P])
        sbkv = at("sbkv", 22016, [P, 2, SEQ])
        tril_s = at("tril_s", 24064, [P, P])
        triu_s = sb("triu_s", [P, P])
        invc = sb("invc", [P, 4, META])
        ych = at("ych", 24576, [P, HEADS, SEQ], F32R)
        ycl = at("ycl", 32768, [P, HEADS, SEQ], F32R)
        ybh = at("ybh", 40960, [P, HEADS, SEQ], F32R)
        ybl = at("ybl", 49152, [P, HEADS, SEQ], F32R)
        msum = at("msum", T0, [P, DB, SEQ])
        mh = at("mh", 0, [P, DB, SEQ], F32R)
        ml = at("ml", T0, [P, DB, SEQ], F32R)

        acc = ctx.enter_context(nc.psum_tensor("acc", [P, 4, 512], F32))
        aux = ctx.enter_context(nc.psum_tensor("aux", [P, 4, 512], F32))
        cos_s, sin_s, kpe, kpe_sq = (tab[:, k, :] for k in range(4))
        kpe_g = quad_b[0:ROPE, 3, :]

        raw_landed = [sem(f"raw_landed{s}") for s in range(RING)]
        hi_ready, lo_ready = sem("hi_ready"), sem("lo_ready")
        chunk_used = sem("chunk_used")
        block_done = sem("block_done")
        bank_free = sem("bank_free")
        vec_landed, consts_landed, eps_ready = sem("vec_landed"), sem("consts_landed"), sem("eps_ready")
        h_landed = [sem(f"h_landed{q}") for q in range(4)]
        xh_ready = sem("xh_ready")
        sq_ready = sem("sq_ready")
        x_ready = sem("x_ready")
        ss_ready, ss_sum, rs_ready = sem("ss_ready"), sem("ss_sum"), sem("rs_ready")
        lat_hi, lat_ready, lat_sum, lat_rs = sem("lat_hi"), sem("lat_ready"), sem("lat_sum"), sem("lat_rs")
        kpe_rot = sem("kpe_rot")
        silu_in, silu_out = sem("silu_in"), sem("silu_out")
        act_hi, act_ready = sem("act_hi"), sem("act_ready")
        bias_landed, bias_masked, bias_free = sem("bias_landed"), sem("bias_masked"), sem("bias_free")
        dist_landed, dist_sum, dist_ready, dist_stored = (
            sem("dist_landed"), sem("dist_sum"), sem("dist_ready"), sem("dist_stored"))
        mask_landed, tables_landed = sem("mask_landed"), sem("tables_landed")
        pool_step, pool_ready = sem("pool_step"), sem("pool_ready")
        yb_hi, gate_out = sem("yb_hi"), sem("gate_out")
        m_sum, m_hi, m_ready = sem("m_sum"), sem("m_hi"), sem("m_ready")
        out_ready, stored = sem("out_ready"), sem("stored")

        STEPS = ("sq", "sums", "rs", "qk", "vtp", "vt", "scores", "sx", "exp", "p", "pt", "ptc", "ptd", "pv", "out", "done")
        S = {k: {s: sem(f"{k}_{s}") for s in STEPS} for k in ("na", "mla", "moba")}
        SB = {s: sem(f"sb_{s}") for s in ("copy", "z", "v", "zs", "ln", "sp", "cum", "u", "exp", "a", "pv", "out", "done")}

        class Att:

            def __init__(self, kind, rows, tiles, keys, scale):
                self.kind, self.rows, self.tiles, self.keys, self.scale = kind, rows, tiles, keys, scale
                self.nq = rows * tiles
                self.kt = [(k // P, k, min(P, keys - k)) for k in range(0, keys, P)]
                self.s = S[kind]

        NA = Att("na", QR, QT, L, float(P) ** -0.5)
        MLA = Att("mla", QR, QT, L, float(MLA_QK) ** -0.5)
        MOBA = Att("moba", P, SEQ // P, SEQ, float(P) ** -0.5)

        AT_CQ = At()
        AT_CKV = AT_CQ.past(CD, 1)
        AT_QUP = AT_CKV.past(CD, 1)
        AT_KVUP = AT_QUP.past(6, 4)
        AT_QKV = AT_KVUP.past(4, 4)
        AT_OUTB = AT_QKV.past(6 * CD, 6)
        AT_OUTA = AT_OUTB.past(4 * CH, 4)
        AT_FFN = AT_OUTA.past(4 * CH, 4)
        AT_DOWN = AT_FFN.past(11 * 2 * CD, 22)
        AT_IN2 = AT_DOWN.past(4 * CF, 4)
        AT_IN2S = AT_IN2.past(6 * CD, 6)
        AT_MERGEA = AT_IN2S.past(8 * CD, 8)
        AT_POOL = AT_MERGEA.past(4 * (CD + CH), 8)
        AT_MERGE = AT_POOL.past(2, 2)
        AT_OUT2 = AT_MERGE.past(4 * 2 * (CD + CH), 16)
        AT_FFN2 = AT_OUT2.past(4 * CD, 4)
        AT_DOWN2 = AT_FFN2.past(11 * 2 * CD, 22)
        AT_END = AT_DOWN2.past(4 * CF, 4)
        assert nc.sbuf_base <= arena
        assert AT_END.n + RING == NCH
        NCONST = 4 * 16
        NA_DMAS = 7

        def flat(ap):
            return ap.rearrange("p e n -> p (e n)")

        block = ctx.enter_context(nc.Block())


        @block.sync
        def _(sp):
            def load(n, slot):
                sp.dma_start(raw[:, slot, :], wts[bass.ds(n, 1)].rearrange("c p f -> p (c f)"))\
                    .then_inc(raw_landed[slot], 16)

            sp.dma_start(vec[:], vecs).then_inc(vec_landed, 16)
            for q in range(4):
                load(q, q)
                sp.dma_start(h[:, 4 * q:4 * q + 4, :], hT[:, 4 * q:4 * q + 4, :]).then_inc(h_landed[q], 16)
            for dst, src in ((ones_s[:], ones), (ident_s[:], ident), (tab[:, 0:2, :], cos_sin), (rot_s[:], rot)):
                sp.dma_start(dst, src).then_inc(consts_landed, 16)
            with sp.Fori(1, NCH // RING) as i:
                for s in range(RING):
                    sp.wait_ge(lo_ready, i * RING + (s + 1 - RING))
                    load(i * RING + s, s)
            for q in range(4):
                sp.wait_ge(out_ready, q + 1)
                sp.dma_start(out[:, 4 * q:4 * q + 4, :], h[:, 4 * q:4 * q + 4, META:L]).then_inc(stored, 16)
            sp.wait_ge(stored, 64)

        @block.gpsimd
        def _(pool):
            pool.dma_start(onehot_s[:], onehot).then_inc(dist_landed, 16)
            pool.dma_start(neg_s[:], neg).then_inc(dist_landed, 16)
            pool.dma_start(relT_s[:], relT).then_inc(dist_landed, 16)
            pool.dma_start(triu_s[:], triu).then_inc(tables_landed, 16)
            pool.dma_start(invc[:], inv_count).then_inc(tables_landed, 16)
            pool.wait_ge(dist_ready, 1)
            pool.dma_start(dist_dram.rearrange("c h d -> h c d"), dist.unsqueeze(1).to_broadcast([HEADS, P, DISTS + 1]))\
                .then_inc(dist_stored, 16)
            pool.wait_ge(chunk_used, AT_QKV.n)
            pool.dma_start(mask_s[0:QR], na_mask).then_inc(mask_landed, 16)
            pool.memset(bias[:], 0.0).then_inc(bias_free, 1)
            pool.wait_ge(mask_landed, 16)
            with pool.Fori(0, HEADS) as i:
                pool.wait_ge(bias_free, i + 1)
                pool.dma_start(bias[0:QR, :, 0:META], bass.AP(meta_b.tensor, i * META, [[0, QR], [0, 3], [1, META]]))\
                    .then_inc(bias_landed, 16)
                for r in range(ROWS):
                    a = 0
                    while a < GRID:
                        q = r * GRID + a + 2
                        n = min(GRID - a, QR - q % QR)
                        src = bass.AP(rp.tensor, i * (RPR * GRID) + (a * HEADS * RPR + 7 - r) * GRID,
                                      [[HEADS * RPR * GRID, n], [GRID, ROWS], [1, GRID]])
                        dst = bias[q % QR:q % QR + n, q // QR, META:L].rearrange("p (r c) -> p r c", c=GRID)
                        pool.dma_start(dst, src).then_inc(bias_landed, 16)
                        a += n
                pool.wait_ge(bias_landed, i * (16 * NA_DMAS) + 16 * NA_DMAS)
                pool.tensor_tensor(bias[0:QR], bias[0:QR], mask_s[0:QR], ALU.add).then_inc(bias_masked, 1)
            pool.wait_ge(dist_stored, 16)
            pool.wait_ge(chunk_used, AT_IN2.n + 1)
            with pool.Fori(0, HEADS) as i:
                pool.wait_ge(bias_free, i + (HEADS + 1))
                for t in range(2):
                    pool.dma_start(bias2[:, t, :],
                                   bass.AP(dist_dram.tensor, i * (DISTS + 1) + (SEQ - 1 - t * P),
                                           [[HEADS * (DISTS + 1) - 1, P], [1, SEQ]])).then_inc(bias_landed, 16)
            pool.wait_ge(MOBA.s["done"], HEADS + 1)
            pool.dma_start(tril_s[:], tril).then_inc(tables_landed, 16)
            pool.wait_ge(bank_free, 4 + 4 * AT_MERGEA.g)
            pool.wait_ge(tables_landed, 48)
            steps = [0]

            def then(ins):
                steps[0] += 1
                ins.then_inc(pool_step, 1)
                pool.wait_ge(pool_step, steps[0])

            for g, w in enumerate(WINDOWS):
                u = qkvu[:, 6 * HEADS + 2 * g:6 * HEADS + 2 * g + 2, :]
                src, step = u, 1
                while step < w:
                    dst = pool_b[:] if step in (2, 8) else pool_a[:]
                    then(pool.tensor_copy(dst[:, :, 0:step], src[:, :, 0:step]))
                    then(pool.tensor_tensor(dst[:, :, step:SEQ], src[:, :, step:SEQ], src[:, :, 0:SEQ - step], ALU.add))
                    src, step = dst, 2 * step
                then(pool.tensor_tensor(src[:, :, 0:META], src[:, :, 0:META],
                                        invc[:, g, :].unsqueeze(1).to_broadcast([P, 2, META]), ALU.mult))
                then(pool.tensor_scalar(src[:, :, META:SEQ], src[:, :, META:SEQ], 1.0 / w, None, ALU.mult))
                then(pool.tensor_tensor(src, src, u, ALU.subtract))
                then(pool.tensor_copy(ph[:, 2 * g:2 * g + 2, :], src))
                then(pool.tensor_tensor(pl[:, 2 * g:2 * g + 2, :], src, ph[:, 2 * g:2 * g + 2, :].bitcast(F32),
                                        ALU.subtract))
            pool.sem_inc(pool_ready, 1)

        @block.scalar
        def _(act):
            def high_part(at, j):
                j += AHEAD
                act.wait_ge(raw_landed[slot_of(at, j)], loads_of_slot(at, j) * 16)
                if not (isinstance(at, At) and at.n + j < RING):
                    act.wait_ge(chunk_used, chunks_behind(at, j - RING + 1))
                act.activation(whi[:, slot_of(at, j), :], raw[:, slot_of(at, j), :], ACT.Copy).then_inc(hi_ready, 1)

            def high_parts(at, count, first=0):
                for j in range(first, count):
                    high_part(at, j)

            def inv_rms(dst, src, n_features, wait, wait_n, done):
                act.wait_ge(wait, wait_n)
                act.activation(dst, src, ACT.Ln, scale=1.0 / n_features, bias=eps_s[:, 0:1])
                act.drain()
                act.activation(dst, dst, ACT.Exp, scale=-0.5).then_inc(done, 1)

            def residual(at, b0, gain, cols, dst_cols, chunks, first=0):
                high_parts(at, chunks, first)
                for ob in range(4):
                    act.wait_ge(bank_free, groups_behind(at, 4, 4 + ob + 1))
                    if gain is not None:
                        act.activation(xh[:, bass.ds(b0 + ob, 1), dst_cols], h[:, bass.ds(b0 + ob, 1), cols],
                                       ACT.Copy, scale=vec[:, bass.ds(b0 + (VEC[gain] + ob), 1)])\
                            .then_inc(xh_ready, 1)
                n = cols.stop - cols.start
                act.activation(quad_b[:, :, 0:n], h[:, bass.ds(b0, 4), cols], ACT.Square).then_inc(sq_ready, 1)

            def exponentials(a, hd):
                act.wait_ge(a.s["sx"], hd + 1)
                src, scale = (aux, a.scale) if a is MLA else (sx, 1.0)
                for t in range(a.tiles):
                    last = act.activation(sx[0:a.rows, t, 0:a.keys], src[0:a.rows, t, 0:a.keys], ACT.Exp,
                                          bias=small[0:a.rows, 0, t:t + 1], scale=scale,
                                          accum_out=small[0:a.rows, 1, t:t + 1])
                last.then_inc(a.s["exp"], 1)

            def copy_transposed(a, hd):
                act.wait_ge(a.s["pt"], hd + 1)
                act.activation(pt[:, 0:2, 0:a.nq], aux[:, 0:2, 0:a.nq], ACT.Copy).then_inc(a.s["ptc"], 1)

            def copy_values_transposed(a):
                act.activation(flat(vt[:, 0:2, :]), aux[:, 3, 0:2 * P], ACT.Copy)
                act.activation(vt[0:META, 2, :], aux[0:META, 3, 2 * P:3 * P], ACT.Copy).then_inc(a.s["vt"], 1)

            def outputs(a, hd, dst, gain):
                act.wait_ge(a.s["pv"], hd + 1)
                act.activation(flat(dst[:, bass.ds(hd, 1), 0:NQ]), aux[:, 3, 0:NQ], ACT.Copy,
                               scale=vec[:, bass.ds(hd + gain, 1)])
                act.activation(osq[:], aux[:, 3, 0:NQ], ACT.Square).then_inc(a.s["out"], 1)

            def mla_squares(hd):
                act.activation(sq2[:, 0, :], flat(qnope[:, bass.ds(hd, 1), :]), ACT.Square)
                act.activation(sq2[:, 1, :], flat(knope[:, bass.ds(hd, 1), :]), ACT.Square)
                act.activation(sqr[:], flat(qrope[:, bass.ds(hd, 1), :]), ACT.Square)
                act.activation(qg[:], flat(qrope[:, bass.ds(hd, 1), :]), ACT.Copy,
                               scale=vec[0:ROPE, VEC["q_rope_g"]:VEC["q_rope_g"] + 1])
                act.activation(vc[:], flat(vmla[:, bass.ds(hd, 1), :]), ACT.Copy).then_inc(MLA.s["sq"], 1)

            act.wait_ge(vec_landed, 16)
            act.wait_ge(eps_ready, 1)
            high_parts(At(-AHEAD, 0), AHEAD)
            for q in range(4):
                act.wait_ge(h_landed[q], 16)
                if q:
                    act.wait_ge(x_ready, q)
                for b in range(4 * q, 4 * q + 4):
                    act.activation(xh[:, b, :], h[:, b, :], ACT.Copy, scale=vec[:, VEC["mix_g"] + b:VEC["mix_g"] + b + 1])\
                        .then_inc(xh_ready, 1)
                act.activation(quad_b[:, :, :], h[:, 4 * q:4 * q + 4, :], ACT.Square).then_inc(sq_ready, 1)
                high_part(AT_CQ, 2 * q)
                high_part(AT_CQ, 2 * q + 1)
            inv_rms(rstd[:], aux[:, 3, 0:L], D, ss_sum, 1, rs_ready)

            def latent(at, k0, blocks, gain):
                act.wait_ge(bank_free, groups_behind(at, 4, 4 + 4))
                for k in range(blocks):
                    act.activation(lath[:, k0 + k, :], quad_a[:, k, :], ACT.Copy, scale=vec[:, gain + k:gain + k + 1])
                return act.activation(quad_b[:, 0:blocks, :], quad_a[:, 0:blocks, :], ACT.Square)

            latent(AT_CQ, 0, CQB, VEC["cq_g"]).then_inc(lat_hi, 1)
            high_parts(AT_CKV, 4)
            inv_rms(rs_a[:], aux[:, 3, 0:L], CQB * P, lat_sum, 1, lat_rs)
            for j in range(4, CD):
                high_part(AT_CKV, j)
            latent(AT_CKV, CQB, CKVB, VEC["ckv_g"])
            act.activation(kpe_g, kpe, ACT.Copy, scale=vec[0:ROPE, VEC["k_rope_g"]:VEC["k_rope_g"] + 1])
            act.activation(kpe_sq, kpe, ACT.Square).then_inc(lat_hi, 1)
            for g, c in enumerate((2, 2, 1, 1)):
                high_parts(AT_QUP.past(sum((2, 2, 1, 1)[:g]), g), c)
            inv_rms(rs_b[:], aux[:, 3, 0:L], CKVB * P, lat_sum, 2, lat_rs)
            for g in range(4):
                high_parts(AT_KVUP.past(g, g), 1)

            act.wait_ge(dist_ready, 1)
            act.wait_ge(bank_free, 4 + 4 * AT_QKV.g)
            with act.Fori(0, 2) as i:
                at = Turn(AT_QKV, i, 3 * CD, 3)
                for j in range(3 * CD):
                    hd, step = i * 4 + j // 6, j % 6
                    if step == 0:
                        mla_squares(hd)
                    high_part(at, j)
                    if step == 0:
                        inv_rms(sq2[:], aux[:, 0:2, 0:L], MLA_QK, MLA.s["sums"], hd + 1, MLA.s["rs"])
                        copy_values_transposed(MLA)
                    elif step == 3:
                        exponentials(MLA, hd)
                    elif step == 4:
                        copy_transposed(MLA, hd)
                    elif step == 5:
                        outputs(MLA, hd, mixbh, VEC["out_g"] + HEADS)
            def na_squares(hd):
                act.activation(sq2[:], qkv[:, 0:2 * HEADS, :].rearrange("p (s e) n -> p s e n", e=HEADS)
                               [:, :, bass.ds(hd, 1), :].rearrange("p s e n -> p s (e n)"), ACT.Square)
                act.activation(vc[:], flat(qkv[:, bass.ds(hd + 2 * HEADS, 1), :]), ACT.Copy).then_inc(NA.s["sq"], 1)

            def na_turn(at, i, last):
                for k in range(2):
                    hd = i * 2 + k
                    inv_rms(sq2[:], aux[:, 0:2, 0:L], P, NA.s["sums"], hd + 1, NA.s["rs"])
                    high_part(at, 2 * k)
                    exponentials(NA, hd)
                    act.wait_ge(NA.s["vtp"], hd + 1)
                    copy_values_transposed(NA)
                    high_part(at, 2 * k + 1)
                    copy_transposed(NA, hd)
                    if not (last and k == 1):
                        na_squares(hd + 1)
                    outputs(NA, hd, mixah, VEC["out_g"])

            na_squares(0)
            inv_rms(rs_b[:, 0:NQ], aux[:, 3, Q0:L], HEADS * P, ss_sum, 2, rs_ready)
            with act.Fori(0, 3) as i:
                na_turn(Turn(AT_OUTB, i, CH, 1), i, False)
            na_turn(AT_OUTB.past(3 * CH, 3), 3, True)
            high_parts(AT_OUTA, 2)
            inv_rms(rs_a[:, 0:NQ], aux[:, 3, Q0:L], HEADS * P, ss_sum, 3, rs_ready)
            residual(AT_OUTA, 0, "ffn_g", slice(Q0, L), slice(Q0, L), CH, 2)
            with act.Fori(1, 4) as i:
                residual(Turn(AT_OUTA, i, CH, 1), i * 4, "ffn_g", slice(Q0, L), slice(Q0, L), CH)

            def norm_in_first_group(at, k):
                high_parts(at, CD - 1)
                inv_rms(rstd[:], aux[:, 3, 0:L], D, ss_sum, k, rs_ready)
                high_part(at, CD - 1)

            def ffn(start, turn0, k, before_silu):
                def turn(at, i, first):
                    norm_in_first_group(at, k) if first else high_parts(at, CD)
                    high_parts(shifted(at, CD, 1), before_silu)
                    act.wait_ge(silu_in, i + (turn0 + 1))
                    act.activation(quad_b[:, :, 0:SEQ], quad_b[:, :, 0:SEQ], ACT.Silu).then_inc(silu_out, 1)
                    high_parts(shifted(at, CD, 1), CD, before_silu)
                    act.wait_ge(bank_free, groups_behind(at, 4, 4 + 8))
                    act.activation(acth[:, bass.ds(i * 4, 4), :], quad_a[:, :, 0:SEQ], ACT.Copy).then_inc(act_hi, 1)

                turn(start, 0, True)
                with act.Fori(1, 11) as i:
                    turn(Turn(start, i, 2 * CD, 2), i, False)

            ffn(AT_FFN, 0, 4, 3)
            with act.Fori(0, 2) as i:
                for k in range(2):
                    residual(shifted(Turn(AT_DOWN, i, 2 * CF, 2), k * CF, k), i * 8 + 4 * k, "mix2_g", slice(META, L),
                             slice(0, SEQ), CF)
            norm_in_first_group(AT_IN2, 5)
            with act.Fori(1, 6) as i:
                high_parts(Turn(AT_IN2, i, CD, 1), CD)

            act.wait_ge(bank_free, 4 + 4 * AT_IN2S.g)
            with act.Fori(0, HEADS) as i:
                at = Turn(AT_IN2S, i, CD, 1)
                act.activation(mq[:], qkvu[:, 0:3 * HEADS, :].rearrange("p (s e) n -> p s e n", e=HEADS)
                               [:, :, bass.ds(i, 1), :].rearrange("p s e n -> p s (e n)"), ACT.Copy)\
                    .then_inc(MOBA.s["qk"], 1)
                for j in range(CD):
                    high_part(at, j)
                    if j == 0:
                        act.wait_ge(MOBA.s["scores"], i + 1)
                        act.activation(flat(vt[:, 0:2, :]), aux[:, 3, 0:2 * P], ACT.Copy).then_inc(MOBA.s["vt"], 1)
                    elif j == 1:
                        exponentials(MOBA, i)
                    elif j == 3:
                        copy_transposed(MOBA, i)
                    elif j == 5:
                        act.wait_ge(MOBA.s["pv"], i + 1)
                        act.activation(flat(yah[:, bass.ds(i, 1), :]), aux[:, 3, 0:SEQ], ACT.Copy).then_inc(MOBA.s["out"], 1)

            def gate(at):
                act.wait_ge(bank_free, groups_behind(at, 4, 4 + 4))
                act.activation(quad_a[:, :, 0:SEQ], quad_a[:, :, 0:SEQ], ACT.Sigmoid).then_inc(gate_out, 1)

            act.wait_ge(MOBA.s["done"], HEADS + 1)
            with act.Fori(0, 4) as i:
                at = Turn(AT_MERGEA, i, CD + CH, 2)
                for j in range(CD + CH):
                    hd, step = i * 2 + j // 6, j % 6
                    if step == 0:
                        act.activation(sbkv[:], qkvu[:, 4 * HEADS:6 * HEADS, :].rearrange("p (s e) n -> p s e n", e=HEADS)
                                       [:, :, bass.ds(hd, 1), :].rearrange("p s e n -> p s (e n)"), ACT.Copy)\
                            .then_inc(SB["copy"], 1)
                    high_part(at, j)
                    if step == 0:
                        act.wait_ge(SB["z"], hd + 1)
                        act.activation(flat(sbv[:]), aux[:, 1, 0:2 * P], ACT.Copy).then_inc(SB["v"], 1)
                        act.wait_ge(SB["zs"], hd + 1)
                        act.activation(sbl[:], sbz[:], ACT.Abs)
                        act.drain()
                        act.activation(sbl[:], sbl[:], ACT.Exp, scale=-1.0)
                        act.drain()
                        act.activation(sbl[:], sbl[:], ACT.Ln, bias=1.0).then_inc(SB["ln"], 1)
                    elif step == 3:
                        act.wait_ge(SB["u"], hd + 1)
                        act.activation(sbl[:], sbz[:], ACT.Exp).then_inc(SB["exp"], 1)
                    elif step == 5:
                        act.wait_ge(SB["pv"], hd + 1)
                        act.activation(flat(ych[:, bass.ds(hd, 1), :]), aux[:, 3, 0:SEQ], ACT.Copy).then_inc(SB["out"], 1)
                    if j == CD - 1:
                        gate(at)
            for g in range(2):
                high_parts(AT_POOL.past(g, g), 1)
                for ob in range(4):
                    if ob < 3:
                        act.wait_ge(block_done, 3 * (AT_POOL.g + g) + ob + 1)
                    else:
                        act.wait_ge(chunk_used, AT_POOL.n + g + 1)
                    if g == 0 and ob == 0:
                        act.wait_ge(SB["done"], HEADS)
                    k = VEC["pool_scale"] + 4 * g + ob
                    act.activation(ybh[:, 4 * g + ob, :], acc[:, ob, 0:SEQ], ACT.Copy, scale=vec[:, k:k + 1])\
                        .then_inc(yb_hi, 1)
            with act.Fori(0, 4) as i:
                for b in range(2):
                    at = shifted(Turn(AT_MERGE, i, 2 * (CD + CH), 4), b * (CD + CH), 2 * b)
                    high_parts(at, CD)
                    gate(at)
                    high_parts(shifted(at, CD, 1), CH)
                act.wait_ge(m_sum, i + 1)
                act.activation(mh[:, bass.ds(i * 4, 4), :], msum[:, bass.ds(i * 4, 4), :], ACT.Copy).then_inc(m_hi, 1)
            with act.Fori(0, 4) as i:
                residual(Turn(AT_OUT2, i, CD, 1), i * 4, "ffn2_g", slice(META, L), slice(0, SEQ), CD)
            ffn(AT_FFN2, 11, 6, 0)
            with act.Fori(0, 2) as i:
                for k in range(2):
                    residual(shifted(Turn(AT_DOWN2, i, 2 * CF, 2), k * CF, k), i * 8 + 4 * k, None, slice(META, L), None,
                             CF)
            inv_rms(rstd[:], aux[:, 3, 0:L], D, ss_sum, 7, rs_ready)

        @block.vector
        def _(dve):
            def low_part(at, j):
                j += AHEAD
                dve.wait_ge(hi_ready, chunks_behind(at, j + 1))
                dve.tensor_tensor(wlo[:, slot_of(at, j), :], raw[:, slot_of(at, j), :],
                                  whi[:, slot_of(at, j), :].bitcast(F32), ALU.subtract).then_inc(lo_ready, 1)

            def low_parts(at, count, first=0):
                for j in range(first, count):
                    low_part(at, j)

            def wait_block(at, chunks, ob):
                if ob < 3:
                    dve.wait_ge(block_done, groups_behind(at, 3, ob + 1))
                else:
                    dve.wait_ge(chunk_used, chunks_behind(at, chunks))

            def times_rms(at, chunks, dst, cols, scale=None, rows=P):
                scale = rstd if scale is None else scale
                n = cols.stop - cols.start
                for ob in range(4):
                    wait_block(at, chunks, ob)
                    dve.tensor_tensor(dst(ob), acc[0:rows, ob, 0:n], scale[0:rows, cols], ALU.mult)\
                        .then_inc(bank_free, 1)

            def add_squares(n):
                for ob in range(4):
                    if ob:
                        dve.drain()
                    last = dve.tensor_tensor(ss[:, L - n:L], ss[:, L - n:L], quad_b[:, ob, 0:n], ALU.add)
                return last

            def residual(at, b0, chunks, gain, cols, dst_cols, xh0, sq0, scale=None, first=0):
                low_parts(at, chunks, first)
                n = cols.stop - cols.start
                for ob in range(4):
                    wait_block(at, chunks, ob)
                    src = acc[:, ob, 0:n]
                    if scale is not None:
                        dve.tensor_tensor(quad_a[:, ob, 0:n], src, scale[:, 0:n], ALU.mult)
                        dve.drain()
                        src = quad_a[:, ob, 0:n]
                    hb = flat(h[:, bass.ds(b0 + ob, 1), cols])
                    dve.tensor_tensor(hb, src, hb, ALU.add).then_inc(bank_free, 1)
                if sq0 is None:
                    return
                for ob in range(4):
                    if gain is None:
                        break
                    dve.wait_ge(xh_ready, xh0(ob + 1))
                    dve.scalar_tensor_tensor(
                        flat(xl[:, bass.ds(b0 + ob, 1), dst_cols]), flat(h[:, bass.ds(b0 + ob, 1), cols]),
                        vec[:, bass.ds(b0 + (VEC[gain] + ob), 1)],
                        flat(xh[:, bass.ds(b0 + ob, 1), dst_cols]).bitcast(F32), ALU.mult, ALU.subtract)
                dve.wait_ge(sq_ready, sq0)
                add_squares(n).then_inc(x_ready, 1)

            def scaled_scores(a, hd, bias=None, bias_ready=None):
                R, T, K = a.rows, a.tiles, a.keys
                dve.wait_ge(a.s["scores"], hd + 1)
                if bias is None:
                    dve.tensor_reduce(small[0:R, 3, 0:T], aux[0:R, 0:T, 0:K], AX_X, ALU.max, negate=True)
                    dve.drain()
                    dve.tensor_scalar(small[0:R, 0, 0:T], small[0:R, 3, 0:T], a.scale, None, ALU.mult)\
                        .then_inc(a.s["sx"], 1)
                    return
                dve.wait_ge(*bias_ready)
                dve.scalar_tensor_tensor(sx[0:R, 0:T, 0:K], aux[0:R, 0:T, 0:K], a.scale, bias[0:R, 0:T, 0:K],
                                         ALU.mult, ALU.add).then_inc(bias_free, 1)
                dve.drain()
                dve.tensor_reduce(small[0:R, 0, 0:T], sx[0:R, 0:T, 0:K], AX_X, ALU.max, negate=True)\
                    .then_inc(a.s["sx"], 1)

            def probabilities(a, hd):
                R, T, K = a.rows, a.tiles, a.keys
                dve.wait_ge(a.s["exp"], hd + 1)
                dve.reciprocal(small[0:R, 2, 0:T], small[0:R, 1, 0:T])
                dve.drain()
                for t in range(T):
                    last = dve.tensor_scalar(sx[0:R, t, 0:K], sx[0:R, t, 0:K], small[0:R, 2, t:t + 1], None, ALU.mult)
                last.then_inc(a.s["p"], 1)

            def copy_transposed(a, hd):
                dve.wait_ge(a.s["pt"], hd + 1)
                dve.tensor_copy(pt[0:META, 2, 0:a.nq], aux[0:META, 2, 0:a.nq]).then_inc(a.s["ptd"], 1)

            def outputs(a, hd, hi, lo, gain):
                dve.wait_ge(a.s["out"], hd + 1)
                dve.scalar_tensor_tensor(flat(lo[:, bass.ds(hd, 1), 0:NQ]), aux[:, 3, 0:NQ], vec[:, bass.ds(hd + gain, 1)],
                                         flat(hi[:, bass.ds(hd, 1), 0:NQ]).bitcast(F32), ALU.mult, ALU.subtract)
                dve.tensor_tensor(ss[:, Q0:L], ss[:, Q0:L], osq[:], ALU.add).then_inc(a.s["done"], 1)

            dve.memset(eps_s[:], EPS)
            dve.memset(ss[:], 0.0)
            dve.drain()
            dve.sem_inc(bank_free, 4)
            dve.sem_inc(eps_ready, 1)
            for a in (MLA, NA, MOBA):
                dve.sem_inc(a.s["done"], 1)
            low_parts(At(-AHEAD, 0), AHEAD)
            dve.wait_ge(vec_landed, 16)
            for q in range(4):
                for b in range(4 * q, 4 * q + 4):
                    dve.wait_ge(xh_ready, b + 1)
                    dve.scalar_tensor_tensor(xl[:, b, :], h[:, b, :], vec[:, VEC["mix_g"] + b:VEC["mix_g"] + b + 1],
                                             xh[:, b, :].bitcast(F32), ALU.mult, ALU.subtract)
                dve.wait_ge(sq_ready, q + 1)
                add_squares(L).then_inc(x_ready, 1)
                low_part(AT_CQ, 2 * q)
                low_part(AT_CQ, 2 * q + 1)
            dve.wait_ge(rs_ready, 1)
            times_rms(AT_CQ, CD, lambda ob: quad_a[:, ob, :], slice(0, L))
            dve.memset(ss[:], 0.0)
            dve.wait_ge(lat_hi, 1)
            for k in range(CQB):
                last = dve.scalar_tensor_tensor(latl[:, k, :], quad_a[:, k, :], vec[:, VEC["cq_g"] + k:VEC["cq_g"] + k + 1],
                                                lath[:, k, :].bitcast(F32), ALU.mult, ALU.subtract)
            last.then_inc(lat_ready, 1)
            low_parts(AT_CKV, CD)
            for k in range(CKVB):
                wait_block(AT_CKV, CD, k)
                dve.tensor_tensor(quad_a[:, k, :], acc[:, k, 0:L], rstd[:], ALU.mult).then_inc(bank_free, 1)
            wait_block(AT_CKV, CD, 3)
            dve.tensor_tensor(kpe, acc[0:ROPE, 2, 0:L], rstd[0:ROPE, :], ALU.mult).then_inc(bank_free, 2)
            dve.wait_ge(lat_hi, 2)
            for k in range(CKVB):
                last = dve.scalar_tensor_tensor(latl[:, CQB + k, :], quad_a[:, k, :],
                                                vec[:, VEC["ckv_g"] + k:VEC["ckv_g"] + k + 1],
                                                lath[:, CQB + k, :].bitcast(F32), ALU.mult, ALU.subtract)
            last.then_inc(lat_ready, 1)
            done = 0
            for g, c in enumerate((2, 2, 1, 1)):
                at = AT_QUP.past(done, g)
                low_parts(at, c)
                if g == 0:
                    dve.wait_ge(lat_rs, 1)
                if g < 2:
                    times_rms(at, c, lambda ob: qnope[:, 4 * g + ob, :], slice(0, L), rs_a)
                else:
                    times_rms(at, c, lambda ob: qrope[:, 4 * (g - 2) + ob, :], slice(0, L), rs_a, ROPE)
                done += c
            dve.wait_ge(kpe_rot, 1)
            dve.tensor_tensor(kpe, aux[0:ROPE, 2, 0:L], sin_s, ALU.mult)
            dve.tensor_tensor(kpe_g, kpe_g, cos_s, ALU.mult)
            dve.drain()
            dve.tensor_tensor(kpe, kpe, kpe_g, ALU.add)
            for g in range(4):
                at = AT_KVUP.past(g, g)
                low_parts(at, 1)
                if g == 0:
                    dve.wait_ge(lat_rs, 2)
                times_rms(at, 1, lambda ob: (knope if g < 2 else vmla)[:, 4 * (g % 2) + ob, :], slice(0, L), rs_b)
            dve.wait_ge(dist_sum, 1)
            dve.tensor_tensor(dist, aux[0:HEADS, 0, 0:DISTS + 1], neg_s[:], ALU.add).then_inc(dist_ready, 1)

            with dve.Fori(0, 2) as i:
                start = Turn(AT_QKV, i, 3 * CD, 3)
                for j in range(3 * CD):
                    hd, step = i * 4 + j // 6, j % 6
                    if j % CD == CD - 1:
                        at = shifted(start, j - CD + 1, j // CD)
                        times_rms(at, CD, lambda ob: flat(qkv[:, bass.ds(i * 12 + (j // CD * 4 + ob), 1), :]), slice(0, L))
                    if step == 1:
                        dve.wait_ge(MLA.s["rs"], hd + 1)
                        dve.scalar_tensor_tensor(qn[:, 0:NQ], flat(qnope[:, bass.ds(hd, 1), Q0:L]),
                                                 vec[:, VEC["q_nope_g"]:VEC["q_nope_g"] + 1], sq2[:, 0, Q0:L],
                                                 ALU.mult, ALU.mult)
                        dve.tensor_tensor(qg[:], qg[:], cos_s, ALU.mult)
                        dve.tensor_tensor(sqr[:], aux[0:ROPE, 2, 0:L], sin_s, ALU.mult)
                        dve.scalar_tensor_tensor(kn[:], flat(knope[:, bass.ds(hd, 1), :]),
                                                 vec[:, VEC["k_nope_g"]:VEC["k_nope_g"] + 1], sq2[:, 1, :],
                                                 ALU.mult, ALU.mult)
                        dve.tensor_tensor(kr[:], kpe, sq2[0:ROPE, 1, :], ALU.mult)
                        dve.drain()
                        dve.tensor_tensor(sqr[:], sqr[:], qg[:], ALU.add)
                        dve.drain()
                        dve.tensor_tensor(qr[:, 0:NQ], sqr[:, Q0:L], sq2[0:ROPE, 0, Q0:L], ALU.mult)\
                            .then_inc(MLA.s["qk"], 1)
                    low_part(start, j)
                    if step == 2:
                        scaled_scores(MLA, hd)
                    elif step == 3:
                        probabilities(MLA, hd)
                    elif step == 4:
                        copy_transposed(MLA, hd)
                    elif step == 5:
                        outputs(MLA, hd, mixbh, mixbl, VEC["out_g"] + HEADS)
            dve.drain()
            dve.sem_inc(ss_ready, 1)
            dve.wait_ge(rs_ready, 2)
            dve.memset(ss[:], 0.0)
            dve.wait_ge(dist_stored, 16)
            with dve.Fori(0, 4) as i:
                at = Turn(AT_OUTB, i, CH, 1)
                for k in range(2):
                    hd = i * 2 + k
                    dve.wait_ge(NA.s["rs"], hd + 1)
                    dve.scalar_tensor_tensor(qn[:, 0:NQ], flat(qkv[:, bass.ds(hd, 1), Q0:L]),
                                             vec[:, VEC["na_q_g"]:VEC["na_q_g"] + 1], sq2[:, 0, Q0:L], ALU.mult, ALU.mult)
                    dve.scalar_tensor_tensor(kn[:], flat(qkv[:, bass.ds(hd + HEADS, 1), :]),
                                             vec[:, VEC["na_k_g"]:VEC["na_k_g"] + 1], sq2[:, 1, :], ALU.mult, ALU.mult)\
                        .then_inc(NA.s["qk"], 1)
                    low_part(at, 2 * k)
                    scaled_scores(NA, hd, bias, (bias_masked, hd + 1))
                    probabilities(NA, hd)
                    low_part(at, 2 * k + 1)
                    copy_transposed(NA, hd)
                    outputs(NA, hd, mixah, mixal, VEC["out_g"])
                for ob in range(4):
                    wait_block(at, CH, ob)
                    dve.tensor_tensor(quad_a[:, ob, 0:NQ], acc[:, ob, 0:NQ], rs_b[:, 0:NQ], ALU.mult).then_inc(bank_free, 1)
                dve.drain()
                hq = h[:, bass.ds(i * 4, 4), Q0:L]
                dve.tensor_tensor(hq, hq, quad_a[:, :, 0:NQ], ALU.add)
            dve.drain()
            dve.sem_inc(ss_ready, 1)
            low_parts(AT_OUTA, 2)
            dve.wait_ge(rs_ready, 3)
            dve.memset(ss[:], 0.0)
            residual(AT_OUTA, 0, CH, "ffn_g", slice(Q0, L), slice(Q0, L), lambda b: DB + b, 5, rs_a, 2)
            with dve.Fori(1, 4) as i:
                residual(Turn(AT_OUTA, i, CH, 1), i * 4, CH, "ffn_g", slice(Q0, L), slice(Q0, L),
                         lambda b: i * 4 + (DB + b), i + 5, rs_a)
            dve.memset(quad_a[:, :, NQ:NQ + 1], 0.0)

            def ffn(start, turn0, k, conv):
                c0 = Q0 if conv else META
                nt = L - c0

                def turn(at, i):
                    low_parts(at, CD)
                    dve.wait_ge(rs_ready, k)
                    times_rms(at, CD, lambda ob: (quad_a if conv else quad_b)[:, ob, 0:nt], slice(c0, L))
                    dve.drain()
                    if conv:
                        for tap in range(3):
                            low_part(shifted(at, CD, 1), tap)
                            if tap:
                                dve.drain()
                            for ob in range(4):
                                w = vec[:, bass.ds(i * 4 + (VEC["conv_w"] + tap * FFB + ob), 1)]
                                src = quad_a[:, ob, 1 + tap:1 + tap + SEQ]
                                if tap == 0:
                                    last = dve.tensor_scalar(quad_b[:, ob, 0:SEQ], src, w,
                                                             vec[:, bass.ds(i * 4 + (VEC["conv_b"] + ob), 1)],
                                                             ALU.mult, ALU.add)
                                else:
                                    last = dve.scalar_tensor_tensor(quad_b[:, ob, 0:SEQ], src, w, quad_b[:, ob, 0:SEQ],
                                                                    ALU.mult, ALU.add)
                        last.then_inc(silu_in, 1)
                    else:
                        dve.sem_inc(silu_in, 1)
                    at = shifted(at, CD, 1)
                    low_parts(at, CD, 3 if conv else 0)
                    dve.wait_ge(silu_out, i + (turn0 + 1))
                    dve.tensor_tensor(quad_b[:, :, 0:SEQ], quad_b[:, :, 0:SEQ],
                                      rstd[:, META:L].unsqueeze(1).to_broadcast([P, 4, SEQ]), ALU.mult)
                    dve.drain()
                    for ob in range(4):
                        wait_block(at, CD, ob)
                        dve.tensor_tensor(quad_a[:, ob, 0:SEQ], acc[:, ob, 0:SEQ], quad_b[:, ob, 0:SEQ], ALU.mult)\
                            .then_inc(bank_free, 1)
                    dve.wait_ge(act_hi, i + (turn0 + 1))
                    dve.tensor_tensor(actl[:, bass.ds(i * 4, 4), :], quad_a[:, :, 0:SEQ],
                                      acth[:, bass.ds(i * 4, 4), :].bitcast(F32), ALU.subtract).then_inc(act_ready, 1)

                turn(start, 0)
                with dve.Fori(1, 11) as i:
                    turn(Turn(start, i, 2 * CD, 2), i)
                dve.memset(ss[:], 0.0)

            ffn(AT_FFN, 0, 4, True)
            with dve.Fori(0, 2) as i:
                for k in range(2):
                    residual(shifted(Turn(AT_DOWN, i, 2 * CF, 2), k * CF, k), i * 8 + 4 * k, CF, "mix2_g",
                             slice(META, L), slice(0, SEQ), lambda b: i * 8 + (2 * DB + 4 * k + b), i * 2 + (9 + k))
            low_parts(AT_IN2, CD)
            dve.wait_ge(rs_ready, 5)
            times_rms(AT_IN2, CD, lambda ob: qkvu[:, ob, :], slice(META, L))
            dve.memset(ss[:], 0.0)
            with dve.Fori(1, 6) as i:
                at = Turn(AT_IN2, i, CD, 1)
                low_parts(at, CD)
                times_rms(at, CD, lambda ob: flat(qkvu[:, bass.ds(i * 4 + ob, 1), :]), slice(META, L))
            with dve.Fori(0, HEADS) as i:
                at = Turn(AT_IN2S, i, CD, 1)
                for j in range(CD):
                    low_part(at, j)
                    if j == 0:
                        scaled_scores(MOBA, i, bias2, (bias_landed, i * 32 + (16 * NA_DMAS * HEADS + 32)))
                    elif j == 2:
                        probabilities(MOBA, i)
                    elif j == 5:
                        dve.wait_ge(MOBA.s["out"], i + 1)
                        dve.tensor_tensor(flat(yal[:, bass.ds(i, 1), :]), aux[:, 3, 0:SEQ],
                                          flat(yah[:, bass.ds(i, 1), :]).bitcast(F32), ALU.subtract)\
                            .then_inc(MOBA.s["done"], 1)
                times_rms(at, CD, lambda ob: flat(qkvu[:, bass.ds(i * 4 + (3 * HEADS + ob), 1), :]), slice(META, L))

            def gates(at):
                times_rms(at, CD, lambda ob: quad_a[:, ob, 0:SEQ], slice(META, L))

            def branch(at, i, gate_n, dst):
                dve.wait_ge(gate_out, gate_n)
                for ob in range(4):
                    wait_block(at, CH, ob)
                    dve.tensor_tensor(dst(ob), acc[:, ob, 0:SEQ], quad_a[:, ob, 0:SEQ], ALU.mult).then_inc(bank_free, 1)

            dve.wait_ge(tables_landed, 48)
            with dve.Fori(0, 4) as i:
                start = Turn(AT_MERGEA, i, CD + CH, 2)
                for j in range(CD + CH):
                    hd, step = i * 2 + j // 6, j % 6
                    if j == CD - 1:
                        gates(start)
                    if j == CD + CH - 1:
                        branch(shifted(start, CD, 1), i, i + 1, lambda ob: flat(msum[:, bass.ds(i * 4 + ob, 1), :]))
                    low_part(start, j)
                    if step == 0:
                        dve.wait_ge(SB["z"], hd + 1)
                        dve.tensor_scalar(sbz[:], aux[:, 0, 0:SBN], float(P) ** -0.5, None, ALU.mult).then_inc(SB["zs"], 1)
                    elif step == 1:
                        dve.wait_ge(SB["ln"], hd + 1)
                        dve.scalar_tensor_tensor(sbs[:], sbz[:], 0.0, sbl[:], ALU.max, ALU.add)
                        dve.drain()
                        for c in (0, 2 * P):
                            last = dve.tensor_tensor(sbs[:, c:c + P], sbs[:, c:c + P], triu_s[:], ALU.mult)
                        last.then_inc(SB["sp"], 1)
                        dve.scalar_tensor_tensor(sbz[:], sbz[:], 0.0, sbl[:], ALU.min, ALU.subtract)
                        dve.drain()
                    elif step == 3:
                        dve.wait_ge(SB["cum"], hd + 1)
                        dve.tensor_tensor(sbz[:], sbz[:], aux[:, 2, 0:SBN], ALU.subtract).then_inc(SB["u"], 1)
                    elif step == 4:
                        dve.wait_ge(SB["exp"], hd + 1)
                        for c in (0, 2 * P):
                            last = dve.tensor_tensor(sbl[:, c:c + P], sbl[:, c:c + P], triu_s[:], ALU.mult)
                        last.then_inc(SB["a"], 1)
                    elif step == 5:
                        dve.wait_ge(SB["out"], hd + 1)
                        dve.tensor_tensor(flat(ycl[:, bass.ds(hd, 1), :]), aux[:, 3, 0:SEQ],
                                          flat(ych[:, bass.ds(hd, 1), :]).bitcast(F32), ALU.subtract).then_inc(SB["done"], 1)
            for g in range(2):
                low_parts(AT_POOL.past(g, g), 1)
                for ob in range(4):
                    dve.wait_ge(yb_hi, 4 * g + ob + 1)
                    k = VEC["pool_scale"] + 4 * g + ob
                    dve.scalar_tensor_tensor(ybl[:, 4 * g + ob, :], acc[:, ob, 0:SEQ], vec[:, k:k + 1],
                                             ybh[:, 4 * g + ob, :].bitcast(F32), ALU.mult, ALU.subtract)\
                        .then_inc(bank_free, 1)
            with dve.Fori(0, 4) as i:
                for b in range(2):
                    at = shifted(Turn(AT_MERGE, i, 2 * (CD + CH), 4), b * (CD + CH), 2 * b)
                    low_parts(at, CD)
                    gates(at)
                    at = shifted(at, CD, 1)
                    low_parts(at, CH)
                    branch(at, i, i * 2 + (5 + b), lambda ob: quad_b[:, ob, 0:SEQ])
                    dve.drain()
                    mq4 = msum[:, bass.ds(i * 4, 4), :]
                    last = dve.tensor_tensor(mq4, mq4, quad_b[:, :, 0:SEQ], ALU.add)
                last.then_inc(m_sum, 1)
                dve.wait_ge(m_hi, i + 1)
                dve.tensor_tensor(ml[:, bass.ds(i * 4, 4), :], msum[:, bass.ds(i * 4, 4), :],
                                  mh[:, bass.ds(i * 4, 4), :].bitcast(F32), ALU.subtract).then_inc(m_ready, 1)
            with dve.Fori(0, 4) as i:
                residual(Turn(AT_OUT2, i, CD, 1), i * 4, CD, "ffn2_g", slice(META, L), slice(0, SEQ),
                         lambda b: i * 4 + (3 * DB + b), i + 13)
            ffn(AT_FFN2, 11, 6, False)
            with dve.Fori(0, 2) as i:
                for k in range(2):
                    residual(shifted(Turn(AT_DOWN2, i, 2 * CF, 2), k * CF, k), i * 8 + 4 * k, CF, None, slice(META, L),
                             None, None, i * 2 + (17 + k))
            dve.wait_ge(rs_ready, 7)
            for b in range(DB):
                last = dve.scalar_tensor_tensor(h[:, b, META:L], h[:, b, META:L],
                                                vec[:, VEC["final_g"] + b:VEC["final_g"] + b + 1], rstd[:, META:L],
                                                ALU.mult, ALU.mult)
                if b % 4 == 3:
                    last.then_inc(out_ready, 1)

        @block.tensor
        def _(pe):
            def chunk(at, j, chunks, x_hi, x_lo, n, blocks=4, width=P, row=GC, per_chunk=2):
                slot = slot_of(at, j)
                pe.wait_ge(lo_ready, chunks_behind(at, j + 1))
                for ob in range(blocks):
                    if j == 0:
                        pe.wait_ge(bank_free, groups_behind(at, 4, ob + 1))
                    w = ROPE if blocks < 4 and ob == blocks - 1 else width
                    dst = acc[0:w, ob, 0:n]
                    for t in range(per_chunk):
                        c = t * row + ob * width
                        hi, lo = whi[:, slot, c:c + w], wlo[:, slot, c:c + w]
                        kt = j * per_chunk + t
                        pe.matmul(dst, hi, x_hi(kt), start=kt == 0, stop=False)
                        pe.matmul(dst, hi, x_lo(kt), start=False, stop=False)
                        last = pe.matmul(dst, lo, x_hi(kt), start=False, stop=kt == chunks * per_chunk - 1)
                    if j == chunks - 1 and ob < blocks - 1:
                        last.then_inc(block_done, 1 if ob < blocks - 2 else 5 - blocks)
                last.then_inc(chunk_used, 1)

            def group(at, chunks, *args, waits={}, **kwargs):
                for j in range(chunks):
                    if j in waits:
                        pe.wait_ge(*waits[j])
                    chunk(at, j, chunks, *args, **kwargs)

            def token_sums(wait, n_wait):
                pe.wait_ge(wait, n_wait)
                pe.matmul(aux[:, 3, 0:L], ones_s[:], ss[:], start=True, stop=True).then_inc(ss_sum, 1)

            def norm_in_first_group(at, x_hi, x_lo, n, x0):
                for j in range(CD):
                    if j % 2 == 0:
                        pe.wait_ge(x_ready, x0 + j // 2 + 1)
                    chunk(at, j, CD, x_hi, x_lo, n)
                    if j == CD - 2:
                        token_sums(x_ready, x0 + 4)

            def transpose_probabilities(a, hd):
                pe.wait_ge(a.s["p"], hd + 1)
                for t in range(a.tiles):
                    for kt, k, nk in a.kt:
                        last = pe.transpose(aux[0:nk, kt, t * a.rows:(t + 1) * a.rows], sx[0:a.rows, t, k:k + nk],
                                            ident_s[0:a.rows, 0:a.rows])
                last.then_inc(a.s["pt"], 1)

            def weigh_values(a, hd):
                pe.wait_ge(a.s["ptc"], hd + 1)
                if len(a.kt) > 2:
                    pe.wait_ge(a.s["ptd"], hd + 1)
                for kt, k, nk in a.kt:
                    last = pe.matmul(aux[:, 3, 0:a.nq], vt[0:nk, kt, :], pt[0:nk, kt, 0:a.nq], start=kt == 0,
                                     stop=kt == len(a.kt) - 1)
                last.then_inc(a.s["pv"], 1)

            def transpose_values(src, tiles):
                for kt, k, nk in tiles:
                    last = pe.transpose(aux[0:nk, 3, kt * P:kt * P + P], src[:, k:k + nk], ident_s[:])
                return last

            def x1(t):
                return lambda kt: t[:, kt, :]

            def x2(t):
                return lambda kt: t[:, kt, 0:SEQ]

            def xq(t):
                return lambda kt: t[:, kt, 0:NQ]

            for j in range(CD):
                if j % 2 == 0:
                    pe.wait_ge(x_ready, j // 2 + 1)
                chunk(AT_CQ, j, CD, x1(xh), x1(xl), L)
                if j == CD - 2:
                    pe.wait_ge(consts_landed, NCONST)
                    token_sums(x_ready, 4)
            for j in range(CD):
                chunk(AT_CKV, j, CD, x1(xh), x1(xl), L, blocks=3)
                if j == 3:
                    pe.wait_ge(lat_hi, 1)
                    pe.wait_ge(rs_ready, 1)
                    for k in range(CQB):
                        last = pe.matmul(aux[:, 3, 0:L], ones_s[:], quad_b[:, k, :], start=k == 0, stop=k == CQB - 1)
                    last.then_inc(lat_sum, 1)
            pe.wait_ge(lat_ready, 1)
            group(AT_QUP, 2, x1(lath), x1(latl), L)
            group(AT_QUP.past(2, 1), 2, x1(lath), x1(latl), L)
            for g in range(2):
                group(AT_QUP.past(4 + g, 2 + g), 1, x1(lath), x1(latl), L, width=ROPE, row=4 * ROPE, per_chunk=4)
            pe.wait_ge(lat_hi, 2)
            pe.wait_ge(lat_rs, 1)
            for k in range(CKVB):
                last = pe.matmul(aux[:, 3, 0:L], ones_s[:], quad_b[:, k, :], start=k == 0, stop=k == CKVB - 1)
            last.then_inc(lat_sum, 1)
            pe.matmul(aux[0:ROPE, 2, 0:L], rot_s[:], kpe_g, start=True, stop=True).then_inc(kpe_rot, 1)
            pe.wait_ge(lat_ready, 2)
            for g in range(4):
                group(AT_KVUP.past(g, g), 1, lambda kt: lath[:, CQB + kt, :], lambda kt: latl[:, CQB + kt, :], L)
            pe.wait_ge(dist_landed, 48)
            pe.matmul(aux[0:HEADS, 0, 0:DISTS + 1], relT_s[:], onehot_s[:], start=True, stop=True).then_inc(dist_sum, 1)

            with pe.Fori(0, 2) as i:
                start = Turn(AT_QKV, i, 3 * CD, 3)
                for j in range(3 * CD):
                    chunk(shifted(start, j // CD * CD, j // CD), j % CD, CD, x1(xh), x1(xl), L)
                    hd, step = i * 4 + j // 6, j % 6
                    if step == 0:
                        pe.wait_ge(MLA.s["sq"], hd + 1)
                        pe.wait_ge(MLA.s["done"], hd + 1)
                        for k in range(2):
                            pe.matmul(aux[:, k, 0:L], ones_s[:], sq2[:, k, :], start=True, stop=False)
                            pe.matmul(aux[:, k, 0:L], ones_s[0:ROPE, :], sqr[:] if k == 0 else kpe_sq, start=False, stop=True)
                        pe.matmul(aux[0:ROPE, 2, 0:L], rot_s[:], qg[:], start=True, stop=True)
                        transpose_values(vc, MLA.kt).then_inc(MLA.s["sums"], 1)
                    elif step == 2:
                        pe.wait_ge(MLA.s["qk"], hd + 1)
                        for t in range(QT):
                            dst = aux[0:QR, t, 0:L]
                            pe.matmul(dst, qn[:, t * QR:(t + 1) * QR], kn[:], start=True, stop=False)
                            last = pe.matmul(dst, qr[:, t * QR:(t + 1) * QR], kr[:], start=False, stop=True)
                        last.then_inc(MLA.s["scores"], 1)
                    elif step == 4:
                        transpose_probabilities(MLA, hd)
                    elif step == 5:
                        weigh_values(MLA, hd)
            token_sums(ss_ready, 1)
            with pe.Fori(0, 4) as i:
                at = Turn(AT_OUTB, i, CH, 1)
                for k in range(2):
                    hd = i * 2 + k
                    pe.wait_ge(NA.s["sq"], hd + 1)
                    for s in range(2):
                        last = pe.matmul(aux[:, s, 0:L], ones_s[:], sq2[:, s, :], start=True, stop=True)
                    last.then_inc(NA.s["sums"], 1)
                    chunk(at, 2 * k, CH, xq(mixbh), xq(mixbl), NQ)
                    pe.wait_ge(NA.s["qk"], hd + 1)
                    for t in range(QT):
                        last = pe.matmul(aux[0:QR, t, 0:L], qn[:, t * QR:(t + 1) * QR], kn[:], start=True, stop=True)
                    last.then_inc(NA.s["scores"], 1)
                    pe.wait_ge(NA.s["done"], hd + 1)
                    if k == 0:
                        pe.wait_ge(rs_ready, 2)
                    transpose_values(vc, NA.kt).then_inc(NA.s["vtp"], 1)
                    chunk(at, 2 * k + 1, CH, xq(mixbh), xq(mixbl), NQ)
                    transpose_probabilities(NA, hd)
                    weigh_values(NA, hd)
            for j in range(CH):
                pe.wait_ge(NA.s["done"], 2 * j + 3)
                if j == 2:
                    token_sums(ss_ready, 2)
                chunk(AT_OUTA, j, CH, xq(mixah), xq(mixal), NQ)
            with pe.Fori(1, 4) as i:
                group(Turn(AT_OUTA, i, CH, 1), CH, xq(mixah), xq(mixal), NQ)

            def ffn(start, c0, c1, n, x0):
                def turn(at, first):
                    xs = (lambda kt: xh[:, kt, c0:c0 + n], lambda kt: xl[:, kt, c0:c0 + n], n)
                    norm_in_first_group(at, *xs, x0) if first else group(at, CD, *xs)
                    group(shifted(at, CD, 1), CD, lambda kt: xh[:, kt, c1:c1 + SEQ], lambda kt: xl[:, kt, c1:c1 + SEQ],
                          SEQ)

                turn(start, True)
                with pe.Fori(1, 11) as i:
                    turn(Turn(start, i, 2 * CD, 2), False)

            def down(start, a0):
                with pe.Fori(0, 2) as i:
                    for k in range(2):
                        group(shifted(Turn(start, i, 2 * CF, 2), k * CF, k), CF, x1(acth), x1(actl), SEQ,
                              waits={0: (act_ready, a0 + 10), CF - 2: (act_ready, a0 + 11)})

            ffn(AT_FFN, Q0, META, NQ, 4)
            down(AT_DOWN, 0)
            norm_in_first_group(AT_IN2, x2(xh), x2(xl), SEQ, 8)
            with pe.Fori(1, 6) as i:
                group(Turn(AT_IN2, i, CD, 1), CD, x2(xh), x2(xl), SEQ)
            with pe.Fori(0, HEADS) as i:
                at = Turn(AT_IN2S, i, CD, 1)
                for j in range(CD):
                    chunk(at, j, CD, x2(xh), x2(xl), SEQ)
                    if j == 0:
                        pe.wait_ge(MOBA.s["qk"], i + 1)
                        pe.wait_ge(MOBA.s["done"], i + 1)
                        for t in range(2):
                            pe.matmul(aux[:, t, 0:SEQ], mq[:, 0, t * P:(t + 1) * P], mq[:, 1, :], start=True, stop=True)
                        transpose_values(mq[:, 2, :], MOBA.kt).then_inc(MOBA.s["scores"], 1)
                    elif j == 3:
                        transpose_probabilities(MOBA, i)
                    elif j == 5:
                        weigh_values(MOBA, i)
            pe.wait_ge(tables_landed, 48)
            pe.wait_ge(MOBA.s["done"], HEADS + 1)
            with pe.Fori(0, 4) as i:
                start = Turn(AT_MERGEA, i, CD + CH, 2)
                for j in range(CD + CH):
                    if j < CD:
                        chunk(start, j, CD, x2(xh), x2(xl), SEQ)
                    else:
                        chunk(shifted(start, CD, 1), j - CD, CH, x1(yah), x1(yal), SEQ)
                    hd, step = i * 2 + j // 6, j % 6
                    if step == 0:
                        pe.wait_ge(SB["copy"], hd + 1)
                        q = qkvu[:, bass.ds(hd + 3 * HEADS, 1), :]
                        pe.matmul(aux[:, 0, 0:SEQ], sbkv[:, 0, 0:P], flat(q), start=True, stop=True)
                        pe.matmul(aux[:, 0, SEQ:SBN], sbkv[:, 0, P:SEQ],
                                  flat(qkvu[:, bass.ds(hd + 3 * HEADS, 1), P:SEQ]), start=True, stop=True)
                        for t in range(2):
                            last = pe.transpose(aux[:, 1, t * P:(t + 1) * P], sbkv[:, 1, t * P:(t + 1) * P], ident_s[:])
                        last.then_inc(SB["z"], 1)
                    elif step == 3:
                        pe.wait_ge(SB["sp"], hd + 1)
                        pe.matmul(aux[:, 2, 0:SEQ], tril_s[:], sbs[:, 0:SEQ], start=True, stop=False)
                        pe.matmul(aux[:, 2, P:SEQ], ones_s[:], sbs[:, SEQ:SBN], start=False, stop=True)
                        pe.matmul(aux[:, 2, SEQ:SBN], tril_s[:], sbs[:, SEQ:SBN], start=True, stop=True)\
                            .then_inc(SB["cum"], 1)
                    elif step == 5:
                        pe.wait_ge(SB["a"], hd + 1)
                        pe.wait_ge(SB["v"], hd + 1)
                        pe.matmul(aux[:, 3, 0:SEQ], sbv[:, 0, :], sbl[:, 0:SEQ], start=True, stop=False)
                        pe.matmul(aux[:, 3, P:SEQ], sbv[:, 1, :], sbl[:, SEQ:SBN], start=False, stop=True)\
                            .then_inc(SB["pv"], 1)
            pe.wait_ge(pool_ready, 1)
            for g in range(2):
                at = AT_POOL.past(g, g)
                slot = slot_of(at, 0)
                pe.wait_ge(lo_ready, at.n + 1)
                for ob in range(4):
                    pe.wait_ge(bank_free, 4 * at.g + ob + 1)
                    for t in range(2):
                        c = (ob // 2) * 512 + t * 256 + (ob % 2) * P
                        b = 4 * g + 2 * (ob // 2) + t
                        hi, lo = whi[:, slot, c:c + P], wlo[:, slot, c:c + P]
                        pe.matmul(acc[:, ob, 0:SEQ], hi, ph[:, b, :], start=t == 0, stop=False)
                        pe.matmul(acc[:, ob, 0:SEQ], hi, pl[:, b, :], start=False, stop=False)
                        last = pe.matmul(acc[:, ob, 0:SEQ], lo, ph[:, b, :], start=False, stop=t == 1)
                    if ob < 3:
                        last.then_inc(block_done, 1)
                last.then_inc(chunk_used, 1)
            with pe.Fori(0, 4) as i:
                for b, (yh, yl) in enumerate(((ybh, ybl), (ych, ycl))):
                    at = shifted(Turn(AT_MERGE, i, 2 * (CD + CH), 4), b * (CD + CH), 2 * b)
                    group(at, CD, x2(xh), x2(xl), SEQ)
                    group(shifted(at, CD, 1), CH, x1(yh), x1(yl), SEQ)
            with pe.Fori(0, 4) as i:
                group(Turn(AT_OUT2, i, CD, 1), CD, x1(mh), x1(ml), SEQ,
                      waits={j: (m_ready, j // 2 + 1) for j in range(0, CD, 2)})
            ffn(AT_FFN2, 0, 0, SEQ, 12)
            down(AT_DOWN2, 11)
            token_sums(x_ready, 20)


def _blocks(a, n):
    return np.ascontiguousarray(np.asarray(a).reshape(n, P).T)


def _chunks(w, c0, c1, rows=2, width=GC):
    part = w[:, c0:c1]
    if c1 - c0 < width:
        part = np.concatenate([part, np.zeros((w.shape[0], width - (c1 - c0)), w.dtype)], axis=1)
    n = w.shape[0] // (rows * P)
    return part.reshape(n, rows, P, width).transpose(0, 2, 1, 3).reshape(n, P, rows * width)


def _layout(inputs):
    f = {k: np.asarray(v) for k, v in inputs.items()}
    one = {k: f[k][0] for k in ("w_in", "w_q_up", "w_kv_up", "w_out", "w_gate", "w_up", "w_down", "w_in_2", "w_pool_2",
                                "w_br_a_2", "w_br_b_2", "w_br_c_2", "w_out_2", "w_gate_2", "w_up_2", "w_down_2")}
    stream = []

    def groups(w, lo=0, hi=None):
        for c in range(lo, w.shape[1] if hi is None else hi, GC):
            stream.append(_chunks(w, c, c + GC))

    w_in = one["w_in"]
    q_cols = 3 * HEADS * P
    groups(w_in, q_cols, q_cols + CQB * P)
    stream.append(_chunks(w_in, q_cols + CQB * P, w_in.shape[1]))
    q_up = one["w_q_up"].reshape(-1, HEADS, MLA_QK)
    groups(q_up[:, :, :P].reshape(-1, HEADS * P))
    rope_cols = q_up[:, :, P:].reshape(-1, HEADS * ROPE)
    for c in range(0, HEADS * ROPE, 4 * ROPE):
        stream.append(_chunks(rope_cols, c, c + 4 * ROPE, rows=4, width=4 * ROPE))
    kv_up = one["w_kv_up"].reshape(-1, HEADS, 2, P)
    groups(kv_up[:, :, 0].reshape(-1, HEADS * P))
    groups(kv_up[:, :, 1].reshape(-1, HEADS * P))
    groups(w_in, 0, q_cols)
    groups(one["w_out"][HEADS * P:])
    groups(one["w_out"][:HEADS * P])
    for c in range(0, FF, GC):
        groups(one["w_gate"], c, c + GC)
        groups(one["w_up"], c, c + GC)
    groups(one["w_down"])
    w2 = one["w_in_2"]
    groups(w2, 0, q_cols)
    groups(w2, q_cols + HEADS * P, 2 * q_cols + HEADS * P)
    groups(w2, q_cols, q_cols + HEADS * P)
    gates = 2 * q_cols + HEADS * P
    for c in range(0, D, GC):
        groups(w2, gates + c, gates + c + GC)
        groups(one["w_br_a_2"], c, c + GC)
    wp = one["w_pool_2"].reshape(2, 2, 2, P, 2 * P)
    stream.append(wp.transpose(0, 3, 1, 2, 4).reshape(2, P, CE))
    for c in range(0, D, GC):
        for b, name in ((1, "w_br_b_2"), (2, "w_br_c_2")):
            groups(w2, gates + b * D + c, gates + b * D + c + GC)
            groups(one[name], c, c + GC)
    groups(one["w_out_2"])
    for c in range(0, FF, GC):
        groups(one["w_gate_2"], c, c + GC)
        groups(one["w_up_2"], c, c + GC)
    groups(one["w_down_2"])
    stream.append(np.zeros((RING, P, CE), np.float32))
    wts = np.concatenate(stream)

    def column(a, n=P):
        c = np.zeros((P, 1), np.float32)
        c[:n, 0] = a
        return c

    cols = dict(
        mix_g=_blocks(f["mix_norm_g"], DB), ffn_g=_blocks(f["ffn_norm_g"], DB),
        conv_w=_blocks(f["conv_w"], 3 * FFB), conv_b=_blocks(f["conv_b"], FFB),
        cq_g=_blocks(f["mla_cq_g"], CQB), ckv_g=_blocks(f["mla_ckv_g"], CKVB),
        na_q_g=column(f["na_q_g"][0]), na_k_g=column(f["na_k_g"][0]),
        q_nope_g=column(f["mla_q_g"][0, :P]), q_rope_g=column(f["mla_q_g"][0, P:], ROPE),
        k_nope_g=column(f["mla_k_g"][0, :P]), k_rope_g=column(f["mla_k_g"][0, P:], ROPE),
        out_g=np.concatenate([_blocks(f["na_out_g"], HEADS), _blocks(f["mla_out_g"], HEADS)], axis=1),
        mix2_g=_blocks(f["norm_mix_2"], DB), ffn2_g=_blocks(f["norm_ffn_2"], DB),
        final_g=_blocks(f["norm_final_2"], DB), pool_scale=_blocks(f["pool_scale_2"], HEADS))
    assert all(cols[k].shape[1] == n for k, n in VEC_SIZES.items())
    vecs = np.concatenate([cols[k] for k in VEC_SIZES], axis=1)

    tokens = np.concatenate([f["meta_tokens"], f["x"][0]], axis=0)
    hT = tokens.T.reshape(DB, P, L).transpose(1, 0, 2)
    rpb = f["na_rpb"][0]
    rows = np.zeros((HEADS, RPR, RPW), rpb.dtype)
    lo = GRID - 1 - (rpb.shape[2] // 2)
    rows[:, :, lo:lo + rpb.shape[2]] = rpb
    rp = np.stack([rows[:, :, GRID - 1 - c:2 * GRID - 1 - c] for c in range(GRID)])
    return dict(hT=hT, wts=wts, vecs=vecs, rp=rp, meta_b=f["na_meta_bias"][0], relT=f["rel_bias_2"].T, **_constants())


def _constants():
    f4 = np.float32
    i = np.arange(P)
    half = ROPE // 2
    rot = np.zeros((ROPE, ROPE), f4)
    rot[np.arange(half) + half, np.arange(half)] = -1
    rot[np.arange(half), np.arange(half) + half] = 1
    inv = (f4(10000.0) ** (-np.arange(0, ROPE, 2, dtype=f4) / f4(ROPE))).astype(f4)
    ang = np.concatenate([inv, inv])[:, None] * np.arange(L, dtype=f4)[None, :]
    c = np.arange(GRID)
    start = np.clip(c - 8, 0, GRID - 16)
    seen = (c[None] >= start[:, None]) & (c[None] < start[:, None] + 16)
    mask = np.zeros((NQ, L), f4)
    mask[2:, META:] = np.where(np.tile(seen, (ROWS, ROWS)), 0.0, NEG)
    mask[:2, META:] = NEG
    dist = SEQ - 1 - np.arange(DISTS)
    nf = np.maximum(dist, 1).astype(f4)
    large = 16 + (np.log(nf / f4(16)) / f4(np.log(2048 / 16)) * f4(16)).astype(np.int32)
    bucket = np.where(dist < 16, np.maximum(dist, 0), np.minimum(large, BUCKETS - 1))
    onehot = np.zeros((BUCKETS, DISTS + 1), f4)
    causal = dist >= 0
    onehot[bucket[causal], np.arange(DISTS)[causal]] = 1
    neg = np.zeros((HEADS, DISTS + 1), f4)
    neg[:, :DISTS][:, ~causal] = NEG
    count = np.minimum(np.arange(META)[None] + 1, np.array(WINDOWS)[:, None]).astype(f4)
    return dict(ident=np.eye(P, dtype=f4), ones=np.ones((P, P), f4), tril=(i[:, None] > i[None]).astype(f4),
                triu=(i[:, None] < i[None]).astype(f4), rot=rot, cos_sin=np.stack([np.cos(ang), np.sin(ang)], axis=1).astype(f4),
                na_mask=mask.reshape(QT, QR, L).transpose(1, 0, 2), onehot=onehot, neg=neg,
                inv_count=np.broadcast_to(f4(1) / count, (P, len(WINDOWS), META)))


_ARGS = ("hT", "wts", "vecs", "ident", "ones", "tril", "triu", "rot", "cos_sin", "rp", "meta_b", "na_mask", "relT",
         "onehot", "neg", "inv_count")


def kernel(**inputs):
    import concourse.bacc as bacc
    from concourse.bass_utils import run_bass_kernel_spmd

    nc = bacc.Bacc("TRN2", target_bir_lowering=False, num_devices=1)
    given = _layout(inputs)
    arrays, args = {}, []
    for name in _ARGS:
        a = np.ascontiguousarray(given[name])
        arrays[f"in_{name}"] = a
        args.append(nc.dram_tensor(f"in_{name}", a.shape, F32, kind="ExternalInput").ap())
    out = nc.dram_tensor("out_T", (P, DB, SEQ), F32, kind="ExternalOutput").ap()
    build(nc, *args, out)
    r = run_bass_kernel_spmd(nc, [arrays], core_ids=[0])
    got = np.asarray(r.results[0]["out_T"])
    return np.ascontiguousarray(got.transpose(2, 1, 0).reshape(1, SEQ, D))
```
